# Optimizing a Trainium2 kernel written in Bass

```python
import jax, jax.numpy as jnp
from jax import lax
import numpy as np

D_MODEL = 2048
BATCH = 1
SEQ = 256
DEPTH = 2

CHUNK = 64
N_A = DEPTH // 2
N_B = DEPTH - N_A
POOL_WINDOWS = (2, 4, 8, 16)
N_POOL_GROUPS = len(POOL_WINDOWS)
POOL_GC = D_MODEL // N_POOL_GROUPS
HEAD_DIM = 64
N_HEADS = D_MODEL // HEAD_DIM
KV_HEADS = N_HEADS // 8
GROUP = N_HEADS // KV_HEADS
WINDOW = 128
WIN_CHUNKS = WINDOW // CHUNK
ROT_DIM = HEAD_DIM // 4
ROPE_THETA = 500000.0
D_FF = ((8 * D_MODEL // 3 + 255) // 256) * 256
EPS = 1e-5
NEG = -1e30

kernel_name = "yoco_pool_swa_sink_hybrid"

def rmsnorm(x, g):
    xf = x.astype(jnp.float32)
    y = xf * lax.rsqrt(jnp.mean(xf * xf, axis=-1, keepdims=True) + EPS)
    return (y * g.astype(jnp.float32)).astype(x.dtype)

def rope_partial(x, pos):
    half = ROT_DIM // 2
    inv = ROPE_THETA ** (-jnp.arange(half, dtype=jnp.float32) * 2.0 / ROT_DIM)
    ang = pos.astype(jnp.float32)[:, None] * inv[None, :]
    cos = jnp.cos(ang)[None, :, None, :]
    sin = jnp.sin(ang)[None, :, None, :]
    xr = x[..., :ROT_DIM].astype(jnp.float32)
    x1, x2 = xr[..., :half], xr[..., half:]
    rot = jnp.concatenate([x1 * cos - x2 * sin, x2 * cos + x1 * sin], axis=-1)
    return jnp.concatenate([rot.astype(x.dtype), x[..., ROT_DIM:]], axis=-1)

def multiscale_pool(xn):
    B, S, _ = xn.shape
    xg = xn.reshape(B, S, N_POOL_GROUPS, POOL_GC).astype(jnp.float32)
    cs = jnp.pad(lax.cumsum(xg, axis=1), ((0, 0), (1, 0), (0, 0), (0, 0)))
    t1 = jnp.arange(1, S + 1, dtype=jnp.int32)
    outs = []
    for g, w in enumerate(POOL_WINDOWS):
        c = cs[:, :, g]
        lag = jnp.pad(c, ((0, 0), (w, 0), (0, 0)))[:, 1:S + 1]
        cnt = jnp.minimum(t1, w).astype(jnp.float32)[None, :, None]
        outs.append((c[:, 1:] - lag) / cnt)
    pooled = jnp.stack(outs, axis=2)
    return (pooled - xg).astype(xn.dtype)

def swa_sink_attention(q, k, v, sinks):
    B, S, H, Dh = q.shape
    nc = S // CHUNK
    qc = q.reshape(B, nc, CHUNK, KV_HEADS, GROUP, Dh)
    kc = k.reshape(B, nc, CHUNK, KV_HEADS, Dh)
    vc = v.reshape(B, nc, CHUNK, KV_HEADS, Dh)
    pad = ((0, 0), (WIN_CHUNKS - 1, 0), (0, 0), (0, 0), (0, 0))
    kp, vp = jnp.pad(kc, pad), jnp.pad(vc, pad)
    kb = jnp.concatenate([kp[:, o:o + nc] for o in range(WIN_CHUNKS)], axis=2)
    vb = jnp.concatenate([vp[:, o:o + nc] for o in range(WIN_CHUNKS)], axis=2)
    scores = jnp.einsum('bnqhgd,bnkhd->bnhgqk', qc, kb).astype(jnp.float32) * (Dh ** -0.5)
    src_chunk = jnp.arange(nc)[:, None] - (WIN_CHUNKS - 1) + jnp.arange(WINDOW)[None, :] // CHUNK
    valid = src_chunk >= 0
    scores = jnp.where(valid[None, :, None, None, None, :], scores, NEG)
    sink = jnp.broadcast_to(sinks.astype(jnp.float32).reshape(1, 1, KV_HEADS, GROUP, 1, 1),
                            scores.shape[:-1] + (1,))
    probs = jax.nn.softmax(jnp.concatenate([scores, sink], axis=-1), axis=-1)[..., :-1]
    out = jnp.einsum('bnhgqk,bnkhd->bnqhgd', probs.astype(v.dtype), vb)
    return out.reshape(B, S, H * Dh)

def swiglu(x, wg, wu, wd):
    return (jax.nn.silu(x @ wg) * (x @ wu)) @ wd

def setup_inputs(seed: int = 0) -> dict:
    key = jax.random.key(seed)
    ks = jax.random.split(key, 16)
    f32 = jnp.float32
    D, F = D_MODEL, D_FF
    nrm = lambda k, shape, fan: jax.random.normal(k, shape, f32) * (fan ** -0.5)
    gain = lambda k, shape: 1.0 + 0.02 * jax.random.normal(k, shape, f32)
    return {
        "x": jax.random.normal(ks[0], (BATCH, SEQ, D), f32),
        "pool_norm": gain(ks[1], (N_A, D)),
        "pool_w": nrm(ks[2], (N_A, N_POOL_GROUPS, POOL_GC, POOL_GC), POOL_GC),
        "pool_b": 0.02 * jax.random.normal(ks[3], (N_A, N_POOL_GROUPS, POOL_GC), f32),
        "pool_scale": 0.5 + 0.1 * jax.random.normal(ks[4], (N_A, D), f32),
        "kv_norm": gain(ks[5], (D,)),
        "w_kv": nrm(ks[6], (D, 2 * KV_HEADS * HEAD_DIM), D),
        "attn_norm": gain(ks[7], (N_B, D)),
        "w_q": nrm(ks[8], (N_B, D, N_HEADS * HEAD_DIM), D),
        "sinks": jax.random.normal(ks[9], (N_B, N_HEADS), f32),
        "w_o": nrm(ks[10], (N_B, N_HEADS * HEAD_DIM, D), N_HEADS * HEAD_DIM),
        "ffn_norm": gain(ks[11], (DEPTH, D)),
        "w_gate": nrm(ks[12], (DEPTH, D, F), D),
        "w_up": nrm(ks[13], (DEPTH, D, F), D),
        "w_down": nrm(ks[14], (DEPTH, F, D), F),
        "final_norm": gain(ks[15], (D,)),
    }

def reference(x, pool_norm, pool_w, pool_b, pool_scale, kv_norm, w_kv, attn_norm,
              w_q, sinks, w_o, ffn_norm, w_gate, w_up, w_down, final_norm):
    B, S, D = x.shape
    pos = jnp.arange(S, dtype=jnp.int32)
    h = x
    k_sh = v_sh = None
    for layer in range(DEPTH):
        if layer < N_A:
            i = layer
            xn = rmsnorm(h, pool_norm[i])
            pooled = multiscale_pool(xn)
            y = jnp.einsum('bsgc,gce->bsge', pooled, pool_w[i]) + pool_b[i]
            h = h + y.reshape(B, S, D) * pool_scale[i]
        else:
            if k_sh is None:
                kv = rmsnorm(h, kv_norm) @ w_kv
                k_sh = rope_partial(kv[..., :KV_HEADS * HEAD_DIM].reshape(B, S, KV_HEADS, HEAD_DIM), pos)
                v_sh = kv[..., KV_HEADS * HEAD_DIM:].reshape(B, S, KV_HEADS, HEAD_DIM)
            i = layer - N_A
            xn = rmsnorm(h, attn_norm[i])
            q = rope_partial((xn @ w_q[i]).reshape(B, S, N_HEADS, HEAD_DIM), pos)
            h = h + swa_sink_attention(q, k_sh, v_sh, sinks[i]) @ w_o[i]
        h = h + swiglu(rmsnorm(h, ffn_norm[layer]), w_gate[layer], w_up[layer], w_down[layer])
    return rmsnorm(h, final_norm)


_drawn_inputs = setup_inputs


def setup_inputs(seed=0):
    import zlib

    import numpy as np

    out = dict(_drawn_inputs(seed))
    spreads = {}
    factors = {'pool_norm': 5.41,
     'pool_b': 4.382,
     'kv_norm': 8.0,
     'attn_norm': 8.0,
     'sinks': 8.0,
     'ffn_norm': 2.925,
     'final_norm': 2.751}
    for name, (base, spread) in spreads.items():
        noise = np.random.default_rng([zlib.crc32(name.encode()), seed]).standard_normal(out[name].shape)
        drawn = base * np.exp(spread * noise) if base else spread * noise
        out[name] = __import__('jax').numpy.asarray(drawn.astype(out[name].dtype))
    for name, factor in factors.items():
        out[name] = (out[name] * factor).astype(out[name].dtype)
    return out
```

```python
from contextlib import ExitStack

import numpy as np

import concourse.bass as bass
from concourse import mybir


F32 = mybir.dt.float32
F32R = mybir.dt.float32r
ALU = mybir.AluOpType
ACT = mybir.ActivationFunctionType
AX_X = mybir.AxisListType.X

P = 128
D = 2048
S = 256
F = 5632
C = 512
T = S // P
KD = D // P
KF = F // P
NBLK = D // C
NFB = F // C
WINDOWS = (2, 4, 8, 16)
CHUNK = 64
NCH = S // CHUNK
DH = 64
GROUPS = 4
HPG = 8
PAIRS = HPG // 2
ROT = DH // 4
THETA = 500000.0
EPS = 1e-5
SCALE = DH ** -0.5
BANDW = P + max(WINDOWS)
RING = 4

LOADS_D = [(4 * i, 2, 2) for i in range(KD // 4)]
LOADS_F = [(4 * i, 2, 2) for i in range(8)] + [(32 + 3 * i, 2, 1) for i in range(4)]


def units_of(loads):
    out = []
    for k0, a, b in loads:
        out += [(k0, a, 0), (k0 + a, b, a * C)]
    return out


UNITS_D = units_of(LOADS_D)
UNITS_F = units_of(LOADS_F)
UD, UF = len(UNITS_D), len(UNITS_F)

LAP_POOL = 0
LAP_GU = [1, 44]
LAP_DOWN = [23, 66]
LAP_KV = 35
LAP_Q = 36
LAP_O = 40
JOB_GU = [4, 39]
JOB_DOWN = [26, 61]
JOB_KV = 30
JOB_Q = 31
JOB_O = 35
FILL_POOL, HI_POOL = 0, 0
FILL_ACT, HI_ACT = [4, 48], [4, 31]
FILL_DOWN, HI_DOWN = 15, 15
FILL_K = 19
FILL_G = 20
HI_G = 19
FILL_O, HI_O = 44, 27
BLK_DOWN = [4, 12]
BLK_O = 8

O_FIRST = [(0, i) for i in range(6)] + [(1, i) for i in range(6)] + [(0, 6), (0, 7), (1, 6), (1, 7)]

G_POOL, G_FFN0, G_FFN1, G_KV, G_ATTN = range(5)


def trunk(nc, x, pool_w, pool_b, pool_scale, w_kv, w_q, w_o, w_gate, w_up, w_down, final_norm,
          gain_cols, sink_rows, bands, rope, out):
    def rows(w):
        return w.rearrange("(k p) n -> p k n", p=P)

    gate_v = [rows(w_gate[l]) for l in range(2)]
    up_v = [rows(w_up[l]) for l in range(2)]
    down_v = [rows(w_down[l]) for l in range(2)]
    kv_v, q_v, o_v = rows(w_kv), rows(w_q[0]), rows(w_o[0])
    pool_v = [rows(pool_w[0, g]) for g in range(NBLK)]
    x_v = x[0].rearrange("(t p) d -> p t d", p=P)
    out_v = out[0].rearrange("(t p) d -> p t d", p=P)

    with ExitStack() as ctx:
        top = [(nc.sbuf_base + 31) // 32 * 32]

        def at(name, shape, dt, offset):
            return nc.alloc_sbuf_tensor_at(name, shape, dt, offset=offset)

        def place(name, shape, dt):
            size = 4 * int(np.prod(shape[1:]))
            offset = top[0]
            top[0] += (size + 31) // 32 * 32
            return at(name, shape, dt, offset), offset

        h, _ = place("h", [P, T, D], F32)
        hT_hi, o_hi = place("hT_hi", [P, KF, S], F32R)
        hT_lo, o_lo = place("hT_lo", [P, KF, S], F32R)
        xT_hi, o_xhi = place("xT_hi", [P, KD, S], F32R)
        xT_lo, o_xlo = place("xT_lo", [P, KD, S], F32R)
        raw, _ = place("raw", [P, RING, 4 * C], F32)
        w_hi, _ = place("w_hi", [P, RING, 2 * C], F32R)
        w_lo, _ = place("w_lo", [P, RING, 2 * C], F32R)
        act, o_act = place("act", [P, T, C], F32)
        hblk = at("hblk", [P, T, C], F32, o_act)
        sqdump, _ = place("sqdump", [P, C], F32)
        ident, _ = place("ident", [P, P], F32)
        gains, _ = place("gains", [P, 5, KD], F32)
        sink, _ = place("sink", [P, GROUPS * PAIRS], F32)
        nsink, _ = place("nsink", [P, GROUPS * PAIRS], F32)
        ropes, _ = place("ropes", [P, 2, T, ROT], F32)
        sumsq, _ = place("sumsq", [P, T, NBLK], F32)
        total, _ = place("total", [P, T], F32)
        rms, _ = place("rms", [P, T], F32)
        r, _ = place("r", [P, T], F32)
        eps, _ = place("eps", [P, 1], F32)
        mx, _ = place("mx", [P, 2, PAIRS], F32)
        nmax, _ = place("nmax", [P, 2, PAIRS], F32)
        sinkd, _ = place("sinkd", [P, 2, PAIRS], F32)
        esink, _ = place("esink", [P, 2, PAIRS], F32)
        rsum, _ = place("rsum", [P, 2, PAIRS], F32)
        den, _ = place("den", [P, 2, PAIRS], F32)
        rden, _ = place("rden", [P, 2, PAIRS], F32)

        pT_hi, pT_lo = hT_hi[:, 0:KD, :], hT_lo[:, 0:KD, :]
        oT_hi, oT_lo = hT_hi[:, 0:KD, :], hT_lo[:, 0:KD, :]
        free_hi, free_lo = o_hi + 4 * KD * S, o_lo + 4 * KD * S
        xb = at("xb", [P, T, D], F32, free_hi)
        scale_b = at("scale_b", [P, D], F32, free_hi + 4 * T * D)
        bias_b = at("bias_b", [P, D], F32, free_lo)
        band = at("band", [P, len(WINDOWS), BANDW + P], F32, free_lo + 4 * D)
        band_r = at("band_r", [P, len(WINDOWS), BANDW + P], F32, free_lo + 4 * (D + 1088))
        ysc = at("ysc", [P, T, C], F32, free_lo + 4 * (D + 2 * 1088))
        kv = at("kv", [P, T, C], F32, free_hi)
        q = at("q", [P, T, C], F32, free_hi + 4 * 1024)
        rope_a = at("rope_a", [P, T, HPG, ROT], F32, free_hi + 4 * 2048)
        rope_b = at("rope_b", [P, T, HPG, ROT], F32, free_hi + 4 * 2304)
        kT = at("kT", [DH, GROUPS, 3, 2 * CHUNK], F32, free_hi + 4 * 2560)
        qT = at("qT", [DH, NCH, HPG, CHUNK], F32, free_hi + 4 * 4096)
        prob = at("prob", [P, 2, PAIRS, 2 * CHUNK], F32, free_lo)
        probT = at("probT", [P, 2, PAIRS, P], F32, free_lo + 4 * 1024)
        v_mid = at("v_mid", [P, GROUPS * DH], F32, free_lo + 4 * 2048)
        xsq0 = at("xsq0", [P, D], F32, o_xlo)
        xsq1 = at("xsq1", [P, D], F32, o_xhi)
        gfin = at("gfin", [P, D], F32, o_xlo)
        res = at("res", [P, T, D], F32, o_xhi)

        assert top[0] <= nc.sbuf_usable_end, top[0] - nc.sbuf_usable_end
        acc = ctx.enter_context(nc.psum_tensor("acc", [P, 8, C], F32))
        TURN, WORK = 4, 6

        def sem(name):
            return ctx.enter_context(nc.semaphore(name))

        raw_in = [sem(f"raw_in{i}") for i in range(RING)]
        hi_ready = sem("hi_ready")
        unit_ready = sem("unit_ready")
        unit_used = sem("unit_used")
        job_out = sem("job_out")
        t_full = [sem(f"t_full{b}") for b in range(2)]
        t_hi = [sem(f"t_hi{b}") for b in range(2)]
        t_free = [sem(f"t_free{b}") for b in range(2)]
        sq_done = sem("sq_done")
        h_stored = sem("h_stored")
        total_ready = sem("total_ready")
        rms_ready = sem("rms_ready")
        r_ready = sem("r_ready")
        x_in = sem("x_in")
        x_in1 = sem("x_in1")
        band_in, gains_in, small_in, scale_in, gfin_in = (sem(s) for s in (
            "band_in", "gains_in", "small_in", "scale_in", "gfin_in"))
        xsq_act = sem("xsq_act")
        xsq_dve = sem("xsq_dve")
        band_ready = sem("band_ready")
        ident_ready = sem("ident_ready")
        consts_ready = sem("consts_ready")
        xb_ready = sem("xb_ready")
        mix_full = sem("mix_full")
        mix_hi = sem("mix_hi")
        mix_free = sem("mix_free")
        ysc_done = sem("ysc_done")
        rope_step = sem("rope_step")
        kv_ready = sem("kv_ready")
        q_ready = sem("q_ready")
        kT_mid = sem("kT_mid")
        s_full = sem("s_full")
        stat = sem("stat")
        sinkd_ready = sem("sinkd_ready")
        p_exp = sem("p_exp")
        den_step = sem("den_step")
        p_norm = sem("p_norm")
        res_ready = sem("res_ready")
        res_ready1 = sem("res_ready1")
        out_done = sem("out_done")

        def pair_bank(pair, t):
            return acc[:, bass.ds(2 * pair + t, 1), :].rearrange("p a n -> p (a n)")

        block = ctx.enter_context(nc.Block())

        @block.sync
        def _(sp):
            sp.dma_start(h[:, 0, :], x_v[:, 0, :]).then_inc(x_in, 16)
            sp.dma_start(h[:, 1, :], x_v[:, 1, :]).then_inc(x_in1, 16)

            def load(lap, i, w, k0, tiles, col):
                ready = 8 * lap + 2 * i - 2 * RING + 2
                if not isinstance(ready, int) or ready > 0:
                    sp.wait_ge(unit_ready, ready)
                slot = i % RING
                sp.dma_start(raw[:, slot, 0:tiles * C].rearrange("p (k n) -> p k n", k=tiles),
                             w[:, k0:k0 + tiles, bass.ds(col, C)]).then_inc(raw_in[slot], 16)

            def load_gate_up(l, j):
                for m, w in enumerate((gate_v[l], up_v[l])):
                    for i, (k0, a, b) in enumerate(LOADS_D):
                        load(LAP_GU[l] + 2 * j, 4 * m + i, w, k0, a + b, j * C)

            def load_down(l, b):
                for i, (k0, a, c) in enumerate(LOADS_F):
                    load(LAP_DOWN[l] + 3 * b, i, down_v[l], k0, a + c, b * C)

            for g in range(NBLK):
                load(LAP_POOL, g, pool_v[g], 0, 4, 0)
            with sp.Fori(0, NFB) as j:
                load_gate_up(0, j)
            with sp.Fori(0, NBLK) as b:
                load_down(0, b)
            for i, (k0, a, c) in enumerate(LOADS_D):
                load(LAP_KV, i, kv_v, k0, a + c, 0)
            with sp.Fori(0, GROUPS) as g:
                for i, (k0, a, c) in enumerate(LOADS_D):
                    load(LAP_Q + g, i, q_v, k0, a + c, g * C)
            for n in range(0, 16, 2):
                job, i = O_FIRST[n]
                load(LAP_O, n // 2, o_v, 2 * i, 4, job * C)
            with sp.Fori(2, NBLK) as b:
                for i, (k0, a, c) in enumerate(LOADS_D):
                    load(LAP_O + b, i, o_v, k0, a + c, b * C)
            with sp.Fori(0, NFB) as j:
                load_gate_up(1, j)
            with sp.Fori(0, NBLK) as b:
                load_down(1, b)
            for half in range(2):
                cols = slice(half * D // 2, (half + 1) * D // 2)
                sp.wait_ge(res_ready, half + 1)
                sp.dma_start(out_v[:, 0, cols], res[:, 0, cols]).then_inc(out_done, 16)
                sp.wait_ge(res_ready1, half + 1)
                sp.dma_start(out_v[:, 1, cols], res[:, 1, cols]).then_inc(out_done, 16)
            sp.wait_ge(out_done, 4 * 16)

        @block.scalar
        def _(ac):
            def round_hi(lap, i, tiles, off, gain=None, k0=0):
                if i % 2 == 0:
                    ac.wait_ge(raw_in[(i // 2) % RING], 16 * (lap + i // 8 + 1))
                used = 8 * lap + i - RING + 1
                if not isinstance(used, int) or used > 0:
                    ac.wait_ge(unit_used, used)
                slot = raw[:, (i // 2) % RING, off:off + tiles * C]
                if gain is None:
                    nc.scalar.activation(w_hi[:, i % RING, 0:tiles * C], slot, ACT.Copy).then_inc(hi_ready, 1)
                    return
                for kk in range(tiles):
                    last = nc.scalar.activation(w_hi[:, i % RING, kk * C:(kk + 1) * C],
                                                slot[:, kk * C:(kk + 1) * C], ACT.Copy,
                                                scale=gains[:, gain, k0 + kk:k0 + kk + 1])
                last.then_inc(hi_ready, 1)

            def turn_hi(fill, dst, k, gain=None):
                for b in range(2):
                    ac.wait_ge(t_full[b], fill + 1)
                    if gain is None:
                        last = nc.scalar.activation(
                            dst[:, bass.ds(k + 2 * b, 2), :],
                            acc[:, TURN + b, :].rearrange("p (a s) -> p a s", a=2), ACT.Copy)
                    else:
                        for a in range(2):
                            kk = k + 2 * b + a
                            last = nc.scalar.activation(dst[:, kk, :], acc[:, TURN + b, a * S:(a + 1) * S],
                                                        ACT.Copy, scale=gains[:, gain, kk:kk + 1])
                    last.then_inc(t_hi[b], 1)

            def mix_hi_part(g):
                for b in range(2):
                    ac.wait_ge(mix_full, 2 * g + b + 1)
                    for a in range(2):
                        kk = 4 * g + 2 * b + a
                        last = nc.scalar.activation(pT_hi[:, kk, :], acc[:, WORK + b, a * S:(a + 1) * S],
                                                    ACT.Copy, scale=gains[:, G_POOL, kk:kk + 1])
                    last.then_inc(mix_hi, 1)

            def squares(job, c, blk):
                ac.wait_ge(job_out, job + 1)
                for t in range(T):
                    if not isinstance(blk, int) or blk + t > 0:
                        ac.wait_ge(sq_done, 2 * blk + t)
                    nc.scalar.activation(sqdump[:, :], hblk[:, t, :], ACT.Square,
                                         accum_out=sumsq[:, t, bass.ds(c, 1)]).then_inc(sq_done, 1)

            def root(n):
                if n == 0:
                    ac.wait_ge(xsq_act, 1)
                    ac.wait_ge(xsq_dve, 1)
                else:
                    ac.wait_ge(total_ready, n)
                nc.scalar.activation(rms[:, :], total[:, :], ACT.Sqrt, bias=eps[:, :],
                                     scale=1.0 / D).then_inc(rms_ready, 1)

            def gate_out(l, j):
                job = JOB_GU[l] + 2 * j
                ac.wait_ge(unit_used, 8 * (LAP_GU[l] + 2 * j) + UD)
                if isinstance(j, int):
                    ac.wait_ge(r_ready, 2 + 2 * l)
                    ac.wait_ge(h_stored, [4, 12][l])
                for t in range(T):
                    last = nc.scalar.activation(act[:, t, :], acc[:, 2 * (job_pair_gate[l]) + t, :], ACT.Silu,
                                                scale=r[:, t:t + 1])
                last.then_inc(job_out, 1)

            job_pair_gate = [JOB_GU[0] % 2, JOB_GU[1] % 2]

            nc.scalar.dma_start(band[:, :, :], bands).then_inc(band_in, 16)
            nc.scalar.dma_start(gains[:, :, :], gain_cols).then_inc(gains_in, 16)
            nc.scalar.dma_start(scale_b[:, :], pool_scale.partition_broadcast(P)).then_inc(scale_in, 16)
            nc.scalar.dma_start(bias_b[:, :], pool_b.partition_broadcast(P)).then_inc(scale_in, 16)
            nc.scalar.dma_start(sink[:, :], sink_rows).then_inc(small_in, 16)
            nc.scalar.dma_start(ropes[:, :, :, :], rope).then_inc(small_in, 16)
            ac.wait_ge(x_in, 16)
            nc.scalar.activation(xsq0[:, :], h[:, 0, :], ACT.Square,
                                 accum_out=total[:, 0:1]).then_inc(xsq_act, 1)
            ac.wait_ge(consts_ready, 1)
            root(0)
            ac.wait_ge(gains_in, 16)
            for i in range(4):
                round_hi(LAP_POOL, i, 2, (i % 2) * 2 * C)
            mix_hi_part(0)
            mix_hi_part(1)
            for i in range(4, 8):
                round_hi(LAP_POOL, i, 2, (i % 2) * 2 * C)
                if i == 5:
                    mix_hi_part(2)
            turn_hi(FILL_POOL, xT_hi, 0, G_FFN0)
            mix_hi_part(3)
            squares(0, 0, 0)

            def gate_up(l, j, first):
                lap = LAP_GU[l] + 2 * j
                for i in range(2 * UD):
                    k0, tiles, off = UNITS_D[i % UD]
                    round_hi(lap, i, tiles, off)
                    if first and l == 0:
                        if i == 1 or i == 3:
                            c = i // 2 + 1
                            turn_hi(FILL_POOL + c, xT_hi, 4 * c, G_FFN0)
                            squares(c, c, c)
                        if i == 5:
                            turn_hi(FILL_POOL + 3, xT_hi, 12, G_FFN0)
                            squares(3, 3, 3)
                    if first and l == 1 and i == 5:
                        turn_hi(FILL_O + 3, xT_hi, 12, G_FFN1)
                        squares(JOB_O + 3, 3, BLK_O + 3)
                    if first and i == 7:
                        root(1 + 2 * l)
                    if not first and i == 5:
                        turn_hi(FILL_ACT[l] + j - 1, hT_hi, 4 * j - 4)
                    if i == 10:
                        gate_out(l, j)

            def down(l, b, first):
                lap = LAP_DOWN[l] + 3 * b
                for i, (k0, tiles, off) in enumerate(UNITS_F):
                    round_hi(lap, i, tiles, off)
                    if first and i == 5:
                        turn_hi(FILL_ACT[l] + NFB - 1, hT_hi, 4 * NFB - 4)
                        if l == 1:
                            nc.scalar.dma_start(gfin[:, :], final_norm.partition_broadcast(P)).then_inc(gfin_in, 16)
                    if not first and i == 5:
                        if l == 0:
                            turn_hi(FILL_DOWN + b - 1, xT_hi, 4 * b - 4)
                        squares(JOB_DOWN[l] + b - 1, b - 1, BLK_DOWN[l] + b - 1)

            gate_up(0, 0, True)
            with ac.Fori(1, NFB) as j:
                gate_up(0, j, False)
            down(0, 0, True)
            with ac.Fori(1, NBLK) as b:
                down(0, b, False)

            def exps(item):
                g, n = item // NCH, item % NCH
                keys = CHUNK if n == 0 else 2 * CHUNK
                e = n % 2
                ac.wait_ge(sinkd_ready, item + 1)
                if item >= 2:
                    ac.wait_ge(t_full[e], FILL_G + 6 * ((item - 2) // NCH) + 2 + 2 * (((item - 2) % NCH) // 2) + 1)
                nc.scalar.activation(esink[:, e, :], sinkd[:, e, :], ACT.Exp)
                for j in range(PAIRS):
                    last = nc.scalar.activation(prob[:, e, j, 0:keys],
                                                acc[:, WORK + e, j * P:j * P + keys], ACT.Exp,
                                                bias=nmax[:, e, j:j + 1], scale=SCALE,
                                                accum_out=rsum[:, e, j:j + 1])
                last.then_inc(p_exp, 1)

            def q_out(job, dst):
                pair = job % 2
                for t in range(T):
                    last = nc.scalar.activation(dst[:, t, :], acc[:, 2 * pair + t, :], ACT.Copy,
                                                scale=r[:, t:t + 1])
                last.then_inc(job_out, 1)

            def q_turn(g, t):
                ac.wait_ge(t_full[0], FILL_G + 6 * g + t + 1)
                nc.scalar.activation(
                    qT[:, 2 * t:2 * t + 2, 0:4, :].rearrange("d n h s -> d h n s"),
                    acc[0:DH, TURN, :].rearrange("d (h n s) -> d h n s", h=4, n=2),
                    ACT.Copy).then_inc(t_free[0], 1)

            def prob_turn(g, half):
                keys = CHUNK if half == 0 else P
                ac.wait_ge(t_full[0], FILL_G + 6 * g + 2 + 2 * half + 1)
                nc.scalar.activation(probT[0:keys, 0, :, :].rearrange("k a s -> k (a s)"),
                                     acc[0:keys, TURN, :], ACT.Copy).then_inc(t_free[0], 1)

            def o_hi_part(g, half):
                for e in range(2):
                    n = 2 * half + e
                    ac.wait_ge(t_full[e], FILL_G + 6 * g + 3 + 2 * half + 1)
                    nc.scalar.activation(oT_hi[:, PAIRS * g:PAIRS * (g + 1), n * CHUNK:(n + 1) * CHUNK],
                                         acc[:, TURN + e, 0:PAIRS * CHUNK].rearrange("p (a s) -> p a s", a=PAIRS),
                                         ACT.Copy).then_inc(t_hi[e], 1)

            def attention_step(g, s):
                if s == 2:
                    q_turn(g, 0)
                if s == 3:
                    q_turn(g, 1)
                if s == 4:
                    exps(NCH * g)
                    exps(NCH * g + 1)
                if s == 6:
                    prob_turn(g, 0)
                    exps(NCH * g + 2)
                    exps(NCH * g + 3)
                if s == 7:
                    o_hi_part(g, 0)
                if s == 8:
                    prob_turn(g, 1)
                if s == 9:
                    o_hi_part(g, 1)

            for i, (k0, tiles, off) in enumerate(UNITS_D):
                round_hi(LAP_KV, i, tiles, off, G_KV, k0)
                if i == 5:
                    turn_hi(FILL_DOWN + 3, xT_hi, 12)
                    squares(JOB_DOWN[0] + 3, 3, BLK_DOWN[0] + 3)
                if i == 7:
                    root(2)
            for g in range(GROUPS):
                for i, (k0, tiles, off) in enumerate(UNITS_D):
                    round_hi(LAP_Q + g, i, tiles, off, G_ATTN, k0)
                    if i == 2:
                        ac.wait_ge(unit_used, 8 * (LAP_Q + g))
                        if g == 0:
                            ac.wait_ge(r_ready, 3)
                            for half, t in ((0, 1), (1, 0)):
                                tok = slice(half * CHUNK, (half + 1) * CHUNK)
                                nc.scalar.activation(v_mid[tok, :], acc[tok, 2 * (JOB_KV % 2) + t, GROUPS * DH:],
                                                     ACT.Copy, scale=r[tok, t:t + 1])
                            q_out(JOB_KV, kv)
                        else:
                            if g >= 2:
                                ac.wait_ge(t_full[1], FILL_G + 6 * (g - 2) + 2)
                            q_out(JOB_Q + g - 1, q)
                    if g == 0 and i == 6:
                        ac.wait_ge(t_full[0], FILL_K + 1)
                        kT0 = acc[0:DH, TURN, :].rearrange("d (g s) -> d g s", g=GROUPS)
                        nc.scalar.activation(kT[:, :, 0, :], kT0, ACT.Copy)
                        nc.scalar.activation(kT[:, :, 1, CHUNK:], kT0[:, :, CHUNK:], ACT.Copy).then_inc(t_free[0], 1)
                    if g >= 2 and i < 5:
                        attention_step(g - 2, i + 5)
                    if g >= 1 and i >= 5:
                        attention_step(g - 1, i - 3)
            for n, (job, i) in enumerate(O_FIRST):
                k0, tiles, off = UNITS_D[i]
                round_hi(LAP_O, n, tiles, (n % 2) * 2 * C)
                if n == 2:
                    ac.wait_ge(unit_used, 8 * LAP_O)
                    ac.wait_ge(t_full[1], FILL_G + 6 * 2 + 2)
                    q_out(JOB_Q + 3, q)
                if n < 5:
                    attention_step(2, n + 5)
                if n >= 5:
                    attention_step(3, n - 3)
            for b in range(2, NBLK):
                for i, (k0, tiles, off) in enumerate(UNITS_D):
                    round_hi(LAP_O + b, i, tiles, off)
                    c = {(2, 3): 0, (2, 6): 1, (3, 5): 2}.get((b, i))
                    if c is not None:
                        turn_hi(FILL_O + c, xT_hi, 4 * c, G_FFN1)
                        squares(JOB_O + c, c, BLK_O + c)

            gate_up(1, 0, True)
            with ac.Fori(1, NFB) as j:
                gate_up(1, j, False)
            down(1, 0, True)
            with ac.Fori(1, NBLK) as b:
                down(1, b, False)
            squares(JOB_DOWN[1] + 3, 3, BLK_DOWN[1] + 3)
            root(4)
            ac.wait_ge(r_ready, 5)
            ac.wait_ge(h_stored, 4 * NBLK)
            for half in range(2):
                cols = slice(half * D // 2, (half + 1) * D // 2)
                nc.scalar.activation(res[:, 0, cols], h[:, 0, cols], ACT.Copy,
                                     scale=r[:, 0:1]).then_inc(res_ready, 1)

        @block.vector
        def _(ve):
            def split_lo(lap, i, tiles, off, gain=None, k0=0):
                ve.wait_ge(hi_ready, 8 * lap + i + 1)
                slot = raw[:, (i // 2) % RING, off:off + tiles * C]
                if gain is None:
                    nc.vector.tensor_tensor(w_lo[:, i % RING, 0:tiles * C], slot,
                                            w_hi[:, i % RING, 0:tiles * C].bitcast(F32),
                                            ALU.subtract).then_inc(unit_ready, 1)
                    return
                for kk in range(tiles):
                    last = nc.vector.scalar_tensor_tensor(
                        out=w_lo[:, i % RING, kk * C:(kk + 1) * C], in0=slot[:, kk * C:(kk + 1) * C],
                        scalar=gains[:, gain, k0 + kk:k0 + kk + 1],
                        in1=w_hi[:, i % RING, kk * C:(kk + 1) * C].bitcast(F32), op0=ALU.mult, op1=ALU.subtract)
                last.then_inc(unit_ready, 1)

            def lo_of(dst, hi, src, gain, k):
                return nc.vector.scalar_tensor_tensor(out=dst[:, k, :], in0=src, scalar=gains[:, gain, k:k + 1],
                                                      in1=hi[:, k, :].bitcast(F32), op0=ALU.mult,
                                                      op1=ALU.subtract)

            def turn_lo(fill_hi, dst, hi, k, gain=None):
                for b in range(2):
                    ve.wait_ge(t_hi[b], fill_hi + 1)
                    if gain is None:
                        last = nc.vector.tensor_tensor(
                            dst[:, bass.ds(k + 2 * b, 2), :],
                            acc[:, TURN + b, :].rearrange("p (a s) -> p a s", a=2),
                            hi[:, bass.ds(k + 2 * b, 2), :].bitcast(F32), ALU.subtract)
                    else:
                        for a in range(2):
                            last = lo_of(dst, hi, acc[:, TURN + b, a * S:(a + 1) * S], gain, k + 2 * b + a)
                    last.then_inc(t_free[b], 1)

            def mix_lo_part(g):
                for b in range(2):
                    ve.wait_ge(mix_hi, 2 * g + b + 1)
                    for a in range(2):
                        last = lo_of(pT_lo, pT_hi, acc[:, WORK + b, a * S:(a + 1) * S], G_POOL, 4 * g + 2 * b + a)
                    last.then_inc(mix_free, 1)

            def pool_out(g):
                ve.wait_ge(unit_used, 2 * g + 2)
                if g == 0:
                    ve.wait_ge(xb_ready, 2)
                else:
                    hblk_free(g, FILL_POOL + g - 1)
                for t in range(T):
                    nc.vector.tensor_tensor(ysc[:, t, :], acc[:, 2 * (g % 2) + t, :],
                                            scale_b[:, g * C:(g + 1) * C], ALU.mult).then_inc(ysc_done, 1)
                for t in range(T):
                    ve.wait_ge(ysc_done, 2 * g + t + 1)
                    last = nc.vector.tensor_tensor(hblk[:, t, :], ysc[:, t, :], xb[:, t, g * C:(g + 1) * C],
                                                   ALU.add)
                last.then_inc(job_out, 1)

            def hblk_free(blk, fill):
                if fill is not None:
                    ve.wait_ge(t_full[1], fill + 1)
                ve.wait_ge(sq_done, 2 * blk)
                ve.wait_ge(h_stored, blk)

            def residual_out(pair, c, used, blk, fill):
                ve.wait_ge(unit_used, used)
                hblk_free(blk, fill)
                for t in range(T):
                    last = nc.vector.tensor_tensor(hblk[:, t, :], pair_bank(pair, t), h[:, t, bass.ds(c * C, C)],
                                                   ALU.add)
                last.then_inc(job_out, 1)

            def sum_up(blk):
                ve.wait_ge(sq_done, 2 * blk + 2)
                nc.vector.reduce_sum(total[:, :], sumsq[:, :, :], AX_X).then_inc(total_ready, 1)

            def invert(n):
                ve.wait_ge(rms_ready, n + 1)
                nc.vector.reciprocal(r[:, :], rms[:, :]).then_inc(r_ready, 1)

            def up_out(l, j):
                job = JOB_GU[l] + 2 * j + 1
                pair = (JOB_GU[l] + 1) % 2
                ve.wait_ge(unit_used, 8 * (LAP_GU[l] + 2 * j) + 2 * UD)
                ve.wait_ge(job_out, job)
                for t in range(T):
                    last = nc.vector.scalar_tensor_tensor(out=act[:, t, :], in0=acc[:, 2 * pair + t, :],
                                                          scalar=r[:, t:t + 1], in1=act[:, t, :],
                                                          op0=ALU.mult, op1=ALU.mult)
                last.then_inc(job_out, 1)

            nc.vector.memset(eps[:, :], EPS).then_inc(consts_ready, 1)
            ve.wait_ge(x_in1, 16)
            nc.vector.scalar_tensor_tensor(out=xsq1[:, :], in0=h[:, 1, :], scalar=1.0, in1=h[:, 1, :],
                                           op0=ALU.mult, op1=ALU.mult, accum_out=total[:, 1:2]).then_inc(xsq_dve, 1)
            invert(0)
            ve.wait_ge(band_in, 16)
            ve.wait_ge(r_ready, 1)
            nc.vector.tensor_scalar(band_r[:, :, 0:BANDW], band[:, :, 0:BANDW], r[:, 0:1], None, ALU.mult)
            nc.vector.tensor_scalar(band_r[:, :, BANDW:], band[:, :, BANDW:], r[:, 1:2], None,
                                    ALU.mult).then_inc(band_ready, 1)
            ve.wait_ge(gains_in, 16)
            for i in range(4):
                split_lo(LAP_POOL, i, 2, (i % 2) * 2 * C)
            mix_lo_part(0)
            mix_lo_part(1)
            for i in range(4, 8):
                split_lo(LAP_POOL, i, 2, (i % 2) * 2 * C)
                if i == 5:
                    mix_lo_part(2)
                    pool_out(0)
            turn_lo(HI_POOL, xT_lo, xT_hi, 0, G_FFN0)
            mix_lo_part(3)
            pool_out(1)

            def gate_up(l, j, first):
                lap = LAP_GU[l] + 2 * j
                for i in range(2 * UD):
                    k0, tiles, off = UNITS_D[i % UD]
                    split_lo(lap, i, tiles, off)
                    if first and l == 0:
                        if i == 1 or i == 3:
                            c = i // 2 + 1
                            turn_lo(HI_POOL + c, xT_lo, xT_hi, 4 * c, G_FFN0)
                            pool_out(c + 1)
                        if i == 5:
                            turn_lo(HI_POOL + 3, xT_lo, xT_hi, 12, G_FFN0)
                    if first and l == 1:
                        if i == 2:
                            residual_out((JOB_O + 3) % 2, 3, 8 * LAP_GU[1], BLK_O + 3, FILL_O + 2)
                        if i == 5:
                            turn_lo(HI_O + 3, xT_lo, xT_hi, 12, G_FFN1)
                    if first and i == 6:
                        sum_up(3 if l == 0 else BLK_O + 3)
                    if first and i == 8:
                        invert(1 + 2 * l)
                        ve.wait_ge(r_ready, 2 + 2 * l)
                    if not first and i == 2:
                        up_out(l, j - 1)
                    if not first and i == 5:
                        turn_lo(HI_ACT[l] + j - 1, hT_lo, hT_hi, 4 * j - 4)

            def down(l, b, first):
                lap = LAP_DOWN[l] + 3 * b
                for i, (k0, tiles, off) in enumerate(UNITS_F):
                    split_lo(lap, i, tiles, off)
                    if first and i == 2:
                        up_out(l, NFB - 1)
                    if first and i == 5:
                        turn_lo(HI_ACT[l] + NFB - 1, hT_lo, hT_hi, 4 * NFB - 4)
                    if not first and i == 2:
                        pair = (JOB_DOWN[l] + b - 1) % 2
                        residual_out(pair, b - 1, 8 * lap, BLK_DOWN[l] + b - 1,
                                     FILL_DOWN + b - 2 if l == 0 else None)
                    if not first and i == 5 and l == 0:
                        turn_lo(HI_DOWN + b - 1, xT_lo, xT_hi, 4 * b - 4)

            gate_up(0, 0, True)
            with ve.Fori(1, NFB) as j:
                gate_up(0, j, False)
            down(0, 0, True)
            with ve.Fori(1, NBLK) as b:
                down(0, b, False)

            def row_stats(item):
                g, n = item // NCH, item % NCH
                keys = CHUNK if n == 0 else 2 * CHUNK
                e = n % 2
                heads = slice(PAIRS * g, PAIRS * (g + 1))
                ve.wait_ge(s_full, item + 1)
                nc.vector.reduce_max(mx[:, e, :], acc[:, WORK + e, :].rearrange("p (a k) -> p a k", a=PAIRS)[:, :, 0:keys],
                                     AX_X).then_inc(stat, 1)
                ve.wait_ge(stat, 2 * item + 1)
                nc.vector.scalar_tensor_tensor(out=nmax[:, e, :], in0=mx[:, e, :], scalar=-SCALE,
                                               in1=nsink[:, heads], op0=ALU.mult, op1=ALU.min).then_inc(stat, 1)
                ve.wait_ge(stat, 2 * item + 2)
                nc.vector.tensor_tensor(sinkd[:, e, :], sink[:, heads], nmax[:, e, :],
                                        ALU.add).then_inc(sinkd_ready, 1)

            def normalise(item):
                n = item % NCH
                keys = CHUNK if n == 0 else 2 * CHUNK
                e = n % 2
                ve.wait_ge(p_exp, item + 1)
                nc.vector.tensor_tensor(den[:, e, :], rsum[:, e, :], esink[:, e, :], ALU.add).then_inc(den_step, 1)
                ve.wait_ge(den_step, 2 * item + 1)
                nc.vector.reciprocal(rden[:, e, :], den[:, e, :]).then_inc(den_step, 1)
                ve.wait_ge(den_step, 2 * item + 2)
                nc.vector.tensor_tensor(prob[:, e, :, 0:keys], prob[:, e, :, 0:keys],
                                        rden[:, e, :].unsqueeze(2).to_broadcast([P, PAIRS, keys]),
                                        ALU.mult).then_inc(p_norm, 1)

            def q_turn(g, t):
                ve.wait_ge(t_full[1], FILL_G + 6 * g + t + 1)
                nc.vector.tensor_copy(
                    qT[:, 2 * t:2 * t + 2, 4:8, :].rearrange("d n h s -> d h n s"),
                    acc[0:DH, TURN + 1, :].rearrange("d (h n s) -> d h n s", h=4, n=2)).then_inc(t_free[1], 1)

            def prob_turn(g, half):
                ve.wait_ge(t_full[1], FILL_G + 6 * g + 2 + 2 * half + 1)
                nc.vector.tensor_copy(probT[:, 1, :, :].rearrange("k a s -> k (a s)"),
                                      acc[:, TURN + 1, :]).then_inc(t_free[1], 1)

            def o_lo_part(g, half):
                for e in range(2):
                    n = 2 * half + e
                    ve.wait_ge(t_hi[e], HI_G + 2 * g + half + 1)
                    cols = slice(n * CHUNK, (n + 1) * CHUNK)
                    nc.vector.tensor_tensor(oT_lo[:, PAIRS * g:PAIRS * (g + 1), cols],
                                            acc[:, TURN + e, 0:PAIRS * CHUNK].rearrange("p (a s) -> p a s", a=PAIRS),
                                            oT_hi[:, PAIRS * g:PAIRS * (g + 1), cols].bitcast(F32),
                                            ALU.subtract).then_inc(t_free[e], 1)

            def attention_step(g, s):
                if s == 2:
                    q_turn(g, 0)
                if s == 3:
                    q_turn(g, 1)
                if s == 4:
                    row_stats(NCH * g)
                    row_stats(NCH * g + 1)
                    normalise(NCH * g)
                    normalise(NCH * g + 1)
                if s == 6:
                    prob_turn(g, 0)
                    row_stats(NCH * g + 2)
                    row_stats(NCH * g + 3)
                if s == 7:
                    o_lo_part(g, 0)
                    normalise(NCH * g + 2)
                    normalise(NCH * g + 3)
                if s == 8:
                    prob_turn(g, 1)
                if s == 9:
                    o_lo_part(g, 1)

            for i, (k0, tiles, off) in enumerate(UNITS_D):
                split_lo(LAP_KV, i, tiles, off, G_KV, k0)
                if i == 2:
                    residual_out((JOB_DOWN[0] + 3) % 2, 3, 8 * LAP_KV, BLK_DOWN[0] + 3, FILL_DOWN + 2)
                if i == 5:
                    turn_lo(HI_DOWN + 3, xT_lo, xT_hi, 12)
                if i == 6:
                    sum_up(BLK_DOWN[0] + 3)
            for g in range(GROUPS):
                for i, (k0, tiles, off) in enumerate(UNITS_D):
                    split_lo(LAP_Q + g, i, tiles, off, G_ATTN, k0)
                    if g == 0 and i == 0:
                        invert(2)
                    if g == 0 and i == 6:
                        ve.wait_ge(t_full[1], FILL_K + 1)
                        kT1 = acc[0:DH, TURN + 1, :].rearrange("d (g s) -> d g s", g=GROUPS)
                        nc.vector.tensor_copy(kT[:, :, 2, :], kT1)
                        nc.vector.tensor_copy(kT[:, :, 1, 0:CHUNK], kT1[:, :, 0:CHUNK]).then_inc(t_free[1], 1)
                    if g >= 2 and i < 5:
                        attention_step(g - 2, i + 5)
                    if g >= 1 and i >= 5:
                        attention_step(g - 1, i - 3)
            for n, (job, i) in enumerate(O_FIRST):
                k0, tiles, off = UNITS_D[i]
                split_lo(LAP_O, n, tiles, (n % 2) * 2 * C)
                if n < 5:
                    attention_step(2, n + 5)
                if n >= 5:
                    attention_step(3, n - 3)
            for b in range(2, NBLK):
                for i, (k0, tiles, off) in enumerate(UNITS_D):
                    split_lo(LAP_O + b, i, tiles, off)
                    c = {(2, 3): 0, (2, 6): 1, (3, 5): 2}.get((b, i))
                    if c is not None:
                        turn_lo(HI_O + c, xT_lo, xT_hi, 4 * c, G_FFN1)
                    if b == 2 and i == 0:
                        residual_out(JOB_O % 2, 0, 8 * LAP_O + 14, BLK_O, FILL_DOWN + 3)
                    if b == 2 and i == 3:
                        residual_out((JOB_O + 1) % 2, 1, 8 * LAP_O + 16, BLK_O + 1, FILL_O)
                    if b == 3 and i == 2:
                        residual_out((JOB_O + 2) % 2, 2, 8 * (LAP_O + 3), BLK_O + 2, FILL_O + 1)
            gate_up(1, 0, True)
            with ve.Fori(1, NFB) as j:
                gate_up(1, j, False)
            down(1, 0, True)
            with ve.Fori(1, NBLK) as b:
                down(1, b, False)
            residual_out((JOB_DOWN[1] + 3) % 2, 3, 8 * LAP_DOWN[1] + 4 * UF, BLK_DOWN[1] + 3, None)
            sum_up(BLK_DOWN[1] + 3)
            invert(4)
            ve.wait_ge(r_ready, 5)
            ve.wait_ge(h_stored, 4 * NBLK)
            for half in range(2):
                cols = slice(half * D // 2, (half + 1) * D // 2)
                nc.vector.tensor_scalar(res[:, 1, cols], h[:, 1, cols], r[:, 1:2], None,
                                        ALU.mult).then_inc(res_ready1, 1)

        @block.tensor
        def _(te):
            def product(lap, i, at_hi, at_lo, k0, tiles, pair, first, last_unit):
                te.wait_ge(unit_ready, 8 * lap + i + 1)
                w = i % RING
                for kk in range(tiles):
                    k = k0 + kk
                    cols = slice(kk * C, (kk + 1) * C)
                    for t in range(T):
                        tok = slice(t * P, (t + 1) * P)
                        dst = pair_bank(pair, t)
                        end = last_unit and kk == tiles - 1
                        nc.tensor.matmul(dst, at_hi[:, k, tok], w_hi[:, w, cols], start=first and kk == 0, stop=False)
                        nc.tensor.matmul(dst, at_hi[:, k, tok], w_lo[:, w, cols], start=False, stop=False)
                        last = nc.tensor.matmul(dst, at_lo[:, k, tok], w_hi[:, w, cols], start=False, stop=end)
                last.then_inc(unit_used, 1)

            def pair_free(job):
                if not isinstance(job, int) or job >= 2:
                    te.wait_ge(job_out, job - 1)

            def turn(src, fill):
                for b in range(2):
                    if not isinstance(fill, int) or fill > 0:
                        te.wait_ge(t_free[b], fill)
                    for a in range(2):
                        for t in range(T):
                            last = nc.tensor.transpose(acc[:, TURN + b, a * S + t * P:a * S + (t + 1) * P],
                                                       src[:, t, (2 * b + a) * P:(2 * b + a + 1) * P], ident[:, :])
                    last.then_inc(t_full[b], 1)

            def mix(g):
                for b in range(2):
                    if g > 0:
                        te.wait_ge(mix_free, 2 * g)
                    for a in range(2):
                        feats = slice((4 * g + 2 * b + a) * P, (4 * g + 2 * b + a + 1) * P)
                        nc.tensor.matmul(acc[:, WORK + b, a * S:a * S + BANDW], h[:, 0, feats],
                                         band_r[:, g, 0:BANDW], start=True, stop=False, skip_group_check=True)
                        last = nc.tensor.matmul(acc[:, WORK + b, a * S + P:(a + 1) * S], h[:, 1, feats],
                                                band_r[:, g, BANDW:], start=False, stop=True, skip_group_check=True)
                    last.then_inc(mix_full, 1)

            def pool_job(g):
                pair_free(g)
                te.wait_ge(mix_free, 2 * g + 2)
                for u in range(2):
                    product(LAP_POOL, 2 * g + u, pT_hi, pT_lo, 4 * g + 2 * u, 2, g % 2, u == 0, u == 1)

            te.wait_ge(band_ready, 1)
            mix(0)
            mix(1)
            pool_job(0)
            mix(2)
            pool_job(1)
            te.wait_ge(ident_ready, 3)
            te.wait_ge(job_out, 1)
            turn(hblk, FILL_POOL)
            mix(3)
            pool_job(2)
            te.wait_ge(job_out, 2)
            turn(hblk, FILL_POOL + 1)
            pool_job(3)
            te.wait_ge(job_out, 3)
            turn(hblk, FILL_POOL + 2)

            def gate_up(l, j, first):
                lap = LAP_GU[l] + 2 * j
                for m in range(2):
                    job = JOB_GU[l] + 2 * j + m
                    pair_free(job)
                    for u, (k0, tiles, _) in enumerate(UNITS_D):
                        if first and m == 0 and u % 2 == 0:
                            te.wait_ge(t_free[1], [FILL_POOL, FILL_O][l] + u // 2 + 1)
                        product(lap, UD * m + u, xT_hi, xT_lo, k0, tiles, (JOB_GU[l] + m) % 2, u == 0, u == UD - 1)
                        if m == 0 and u == 2:
                            te.wait_ge(job_out, JOB_GU[l] + 2 * j)
                            if first:
                                turn(hblk, [FILL_POOL, FILL_O][l] + 3)
                            else:
                                turn(act, FILL_ACT[l] + j - 1)

            def down(l, b, first):
                job = JOB_DOWN[l] + b
                pair_free(job)
                if first:
                    te.wait_ge(t_free[1], FILL_ACT[l] + NFB - 1)
                for u, (k0, tiles, _) in enumerate(UNITS_F):
                    if first and k0 + tiles > KF - 4:
                        te.wait_ge(t_free[1], FILL_ACT[l] + NFB)
                    product(LAP_DOWN[l] + 3 * b, u, hT_hi, hT_lo, k0, tiles, job % 2, u == 0, u == UF - 1)
                    if u == 2 and first:
                        te.wait_ge(job_out, job)
                        turn(act, FILL_ACT[l] + NFB - 1)
                    if u == 2 and not first and l == 0:
                        te.wait_ge(job_out, job)
                        turn(hblk, FILL_DOWN + b - 1)

            gate_up(0, 0, True)
            with te.Fori(1, NFB) as j:
                gate_up(0, j, False)
            down(0, 0, True)
            with te.Fori(1, NBLK) as b:
                down(0, b, False)

            pair_free(JOB_KV)
            for u, (k0, tiles, _) in enumerate(UNITS_D):
                if u % 2 == 0:
                    te.wait_ge(t_free[1], FILL_DOWN + u // 2 + 1)
                product(LAP_KV, u, xT_hi, xT_lo, k0, tiles, JOB_KV % 2, u == 0, u == UD - 1)
                if u == 2:
                    te.wait_ge(job_out, JOB_KV)
                    turn(hblk, FILL_DOWN + 3)

            def q_turn(g, t):
                for b in range(2):
                    te.wait_ge(t_free[b], FILL_G + 6 * g + t)
                    for a in range(4):
                        head = 4 * b + a
                        last = nc.tensor.transpose(acc[0:DH, TURN + b, a * P:(a + 1) * P],
                                                   q[:, t, head * DH:(head + 1) * DH], ident[:, :])
                    last.then_inc(t_full[b], 1)

            def scores(g, n):
                item, e = NCH * g + n, n % 2
                keys = CHUNK if n == 0 else 2 * CHUNK
                window = max(n - 1, 0)
                if item >= 2:
                    te.wait_ge(p_exp, item - 1)
                for j in range(PAIRS):
                    last = nc.tensor.matmul(acc[:, WORK + e, j * P:j * P + keys],
                                            qT[:, n, 2 * j:2 * j + 2, :].rearrange("d h s -> d (h s)"),
                                            kT[:, g, window, 0:keys], start=True, stop=True)
                last.then_inc(s_full, 1)

            def prob_turn(g, half):
                for e in range(2):
                    n = 2 * half + e
                    keys = CHUNK if n == 0 else 2 * CHUNK
                    te.wait_ge(p_norm, NCH * g + n + 1)
                    te.wait_ge(t_free[e], FILL_G + 6 * g + 2 + 2 * half)
                    for j in range(PAIRS):
                        last = nc.tensor.transpose(acc[0:keys, TURN + e, j * P:(j + 1) * P],
                                                   prob[:, e, j, 0:keys], ident[:, :])
                    last.then_inc(t_full[e], 1)

            def values(g, half):
                for e in range(2):
                    n = 2 * half + e
                    keys = CHUNK if n == 0 else 2 * CHUNK
                    te.wait_ge(t_free[e], FILL_G + 6 * g + 3 + 2 * half)
                    cols = slice(g * DH, (g + 1) * DH)
                    vcols = slice((GROUPS + g) * DH, (GROUPS + g + 1) * DH)
                    v = [kv[0:CHUNK, 0, vcols], kv[:, 0, vcols], v_mid[:, cols], kv[:, 1, vcols]][n]
                    for hh in range(2):
                        last = nc.tensor.matmul(acc[hh * DH:(hh + 1) * DH, TURN + e, 0:PAIRS * CHUNK], v,
                                                probT[0:keys, e, :, hh * CHUNK:(hh + 1) * CHUNK],
                                                start=True, stop=True)
                    last.then_inc(t_full[e], 1)

            def attention_step(g, s):
                if s == 2:
                    te.wait_ge(q_ready, g + 1)
                    q_turn(g, 0)
                if s == 3:
                    q_turn(g, 1)
                if s == 4:
                    for b in range(2):
                        te.wait_ge(t_free[b], FILL_G + 6 * g + 2)
                    scores(g, 0)
                    scores(g, 1)
                if s == 6:
                    prob_turn(g, 0)
                    scores(g, 2)
                    scores(g, 3)
                if s == 7:
                    values(g, 0)
                if s == 8:
                    prob_turn(g, 1)
                if s == 9:
                    values(g, 1)

            for g in range(GROUPS):
                pair_free(JOB_Q + g)
                for u, (k0, tiles, _) in enumerate(UNITS_D):
                    product(LAP_Q + g, u, xT_hi, xT_lo, k0, tiles, (JOB_Q + g) % 2, u == 0, u == UD - 1)
                    if g == 0 and u == 3:
                        te.wait_ge(kv_ready, 1)
                        for t in range(T):
                            te.wait_ge(t_free[t], FILL_K)
                            for a in range(GROUPS):
                                last = nc.tensor.transpose(acc[0:DH, TURN + t, a * P:(a + 1) * P],
                                                           kv[:, t, a * DH:(a + 1) * DH], ident[:, :])
                            last.then_inc(t_full[t], 1)
                    if g >= 2 and u < 2:
                        attention_step(g - 2, u + 8)
                    if g >= 1 and u >= 2:
                        attention_step(g - 1, u)
            for n, (job, u) in enumerate(O_FIRST):
                if u == 0:
                    pair_free(JOB_O + job)
                if n == 0:
                    te.wait_ge(t_free[1], FILL_G + 6 * 1 + 6)
                if u == 4 and job == 0:
                    te.wait_ge(t_free[1], FILL_G + 6 * 2 + 6)
                if n == 12:
                    te.wait_ge(t_free[1], FILL_G + 6 * 3 + 6)
                k0, tiles, _ = UNITS_D[u]
                product(LAP_O, n, oT_hi, oT_lo, k0, tiles, (JOB_O + job) % 2, u == 0, u == UD - 1)
                if n < 2:
                    attention_step(2, n + 8)
                elif n < 10:
                    attention_step(3, n)
            for b in range(2, NBLK):
                pair_free(JOB_O + b)
                for u, (k0, tiles, _) in enumerate(UNITS_D):
                    product(LAP_O + b, u, oT_hi, oT_lo, k0, tiles, (JOB_O + b) % 2, u == 0, u == UD - 1)
                    c = {(2, 0): 0, (2, 3): 1, (3, 2): 2}.get((b, u))
                    if c is not None:
                        te.wait_ge(job_out, JOB_O + c + 1)
                        turn(hblk, FILL_O + c)

            gate_up(1, 0, True)
            with te.Fori(1, NFB) as j:
                gate_up(1, j, False)
            down(1, 0, True)
            with te.Fori(1, NBLK) as b:
                down(1, b, False)

        @block.gpsimd
        def _(gp):
            nc.gpsimd.memset(ident[:, :], 0.0).then_inc(ident_ready, 1)
            gp.wait_ge(ident_ready, 1)
            nc.gpsimd.affine_select(out=ident[:, :], in_=ident[:, :], compare_op=ALU.not_equal, fill=1.0,
                                    base=0, pattern=[[-1, P]], channel_multiplier=1).then_inc(ident_ready, 1)
            gp.wait_ge(scale_in, 32)
            nc.gpsimd.tensor_tensor(bias_b[:, :], bias_b[:, :], scale_b[:, :], ALU.mult).then_inc(xb_ready, 1)
            gp.wait_ge(xb_ready, 1)
            gp.wait_ge(x_in, 16)
            nc.gpsimd.tensor_tensor(xb[:, 0, :], h[:, 0, :], bias_b[:, :], ALU.add)
            gp.wait_ge(x_in1, 16)
            nc.gpsimd.tensor_tensor(xb[:, 1, :], h[:, 1, :], bias_b[:, :], ALU.add).then_inc(xb_ready, 1)
            gp.wait_ge(small_in, 32)
            nc.gpsimd.tensor_scalar(nsink[:, :], sink[:, :], -1.0, None, ALU.mult).then_inc(ident_ready, 1)

            def store(job, c):
                gp.wait_ge(job_out, job + 1)
                nc.gpsimd.tensor_copy(h[:, :, bass.ds(c * C, C)], hblk[:, :, :]).then_inc(h_stored, 1)

            for g in range(NBLK):
                gp.wait_ge(mix_full, 2 * g + 2)
                store(g, g)
            with gp.Fori(0, NBLK) as b:
                store(JOB_DOWN[0] + b, b)

            def rotate(z, heads, n):
                half = ROT // 2
                for t in range(T):
                    zt = z[:, t, 0:heads * DH].rearrange("p (h d) -> p h d", h=heads)
                    cos = ropes[:, 0, t, :].unsqueeze(1).to_broadcast([P, heads, ROT])
                    sin = ropes[:, 1, t, :].unsqueeze(1).to_broadcast([P, heads, ROT])
                    a, b = rope_a[:, t, 0:heads, :], rope_b[:, t, 0:heads, :]
                    nc.gpsimd.tensor_tensor(a, zt[:, :, 0:ROT], cos, ALU.mult)
                    nc.gpsimd.tensor_tensor(b[:, :, 0:half], zt[:, :, half:ROT], sin[:, :, 0:half], ALU.mult)
                    last = nc.gpsimd.tensor_tensor(b[:, :, half:], zt[:, :, 0:half], sin[:, :, half:], ALU.mult)
                last.then_inc(rope_step, 1)
                gp.wait_ge(rope_step, n + 1)
                for t in range(T):
                    zt = z[:, t, 0:heads * DH].rearrange("p (h d) -> p h d", h=heads)
                    last = nc.gpsimd.tensor_tensor(zt[:, :, 0:ROT], rope_a[:, t, 0:heads, :],
                                                   rope_b[:, t, 0:heads, :], ALU.add)
                return last

            gp.wait_ge(job_out, JOB_KV + 1)
            rotate(kv, GROUPS, 0).then_inc(kv_ready, 1)
            for g in range(GROUPS):
                gp.wait_ge(job_out, JOB_Q + g + 1)
                rotate(q, HPG, g + 1).then_inc(q_ready, 1)
            with gp.Fori(0, NBLK) as b:
                store(JOB_O + b, b)
            gp.wait_ge(gfin_in, 16)
            with gp.Fori(0, NBLK) as b:
                gp.wait_ge(job_out, JOB_DOWN[1] + b + 1)
                nc.gpsimd.tensor_tensor(h[:, :, bass.ds(b * C, C)], hblk[:, :, :],
                                        gfin[:, bass.ds(b * C, C)].unsqueeze(1).to_broadcast([P, T, C]),
                                        ALU.mult).then_inc(h_stored, 1)


def band_matrices():
    m = np.zeros((P, len(WINDOWS), BANDW + P), np.float32)
    for g, w in enumerate(WINDOWS):
        for t in range(P):
            for s in range(t, t + w):
                m[t, g, s] = np.float32(1) / np.float32(min(s + 1, w))
                if s - 0 < P:
                    m[t, g, BANDW + s] = np.float32(1) / np.float32(w)
            m[t, g, t] -= np.float32(1)
            m[t, g, BANDW + t] -= np.float32(1)
    return m


def rope_tables():
    half = ROT // 2
    inv = np.float32(THETA) ** (-np.arange(half, dtype=np.float32) * np.float32(2.0) / np.float32(ROT))
    ang = (np.arange(S, dtype=np.float32)[:, None] * inv.astype(np.float32)[None, :]).astype(np.float32)
    cos, sin = np.cos(ang.astype(np.float64)), np.sin(ang.astype(np.float64))
    both = np.stack([np.concatenate([cos, cos], 1), np.concatenate([-sin, sin], 1)]).astype(np.float32)
    return np.ascontiguousarray(both.reshape(2, T, P, ROT).transpose(2, 0, 1, 3))


def kernel(x, pool_norm, pool_w, pool_b, pool_scale, kv_norm, w_kv, attn_norm, w_q, sinks, w_o,
           ffn_norm, w_gate, w_up, w_down, final_norm):
    import concourse.bacc as bacc
    from concourse.bass_utils import run_bass_kernel_spmd

    gains = [pool_norm[0], ffn_norm[0], ffn_norm[1], kv_norm, attn_norm[0]]
    by_head = np.asarray(sinks).reshape(GROUPS * PAIRS, 2).T
    arrays = {
        "x": x, "pool_w": pool_w, "pool_b": np.asarray(pool_b).reshape(1, D), "pool_scale": pool_scale,
        "w_kv": w_kv, "w_q": w_q, "w_o": w_o, "w_gate": w_gate, "w_up": w_up, "w_down": w_down,
        "final_norm": np.asarray(final_norm).reshape(1, D),
        "gain_cols": np.stack([np.asarray(g).reshape(KD, P).T for g in gains], axis=1),
        "sink_rows": np.repeat(by_head, CHUNK, axis=0),
        "bands": band_matrices(), "rope": rope_tables(),
    }
    arrays = {n + "_in": np.ascontiguousarray(a) for n, a in arrays.items()}
    nc = bacc.Bacc("TRN2", target_bir_lowering=False, num_devices=1)
    args = {n[:-3]: nc.dram_tensor(n, a.shape, mybir.dt.from_np(a.dtype), kind="ExternalInput").ap()
            for n, a in arrays.items()}
    args["pool_b"], args["pool_scale"], args["final_norm"] = (
        args[n][0] for n in ("pool_b", "pool_scale", "final_norm"))
    out = nc.dram_tensor("out", (1, S, D), F32, kind="ExternalOutput").ap()
    trunk(nc, out=out, **args)
    return run_bass_kernel_spmd(nc, [arrays], core_ids=[0]).results[0]["out"]
```

```python
from contextlib import ExitStack

import numpy as np

import concourse.bass as bass
from concourse import mybir


F32 = mybir.dt.float32
F32R = mybir.dt.float32r
ALU = mybir.AluOpType
ACT = mybir.ActivationFunctionType
AX_X = mybir.AxisListType.X

P = 128
D = 2048
S = 256
F = 5632
C = 512
T = S // P
KD = D // P
KF = F // P
NBLK = D // C
NFB = F // C
WINDOWS = (2, 4, 8, 16)
CHUNK = 64
NCH = S // CHUNK
DH = 64
GROUPS = 4
HPG = 8
PAIRS = HPG // 2
ROT = DH // 4
THETA = 500000.0
EPS = 1e-5
SCALE = DH ** -0.5
BANDW = P + max(WINDOWS)
RING = 4

LOADS_D = [(4 * i, 2, 2) for i in range(KD // 4)]
LOADS_F = [(4 * i, 2, 2) for i in range(8)] + [(32 + 3 * i, 2, 1) for i in range(4)]


def units_of(loads):
    out = []
    for k0, a, b in loads:
        out += [(k0, a, 0), (k0 + a, b, a * C)]
    return out


UNITS_D = units_of(LOADS_D)
UNITS_F = units_of(LOADS_F)
UD, UF = len(UNITS_D), len(UNITS_F)

LAP_POOL = 0
LAP_GU = [1, 44]
LAP_DOWN = [23, 66]
LAP_KV = 35
LAP_Q = 36
LAP_O = 40
JOB_GU = [4, 39]
JOB_DOWN = [26, 61]
JOB_KV = 30
JOB_Q = 31
JOB_O = 35
FILL_POOL, HI_POOL = 0, 0
FILL_ACT, HI_ACT = [4, 48], [4, 31]
FILL_DOWN, HI_DOWN = 15, 15
FILL_K = 19
FILL_G = 20
HI_G = 19
FILL_O, HI_O = 44, 27
BLK_DOWN = [4, 12]
BLK_O = 8

O_FIRST = [(0, i) for i in range(6)] + [(1, i) for i in range(6)] + [(0, 6), (0, 7), (1, 6), (1, 7)]

G_POOL, G_FFN0, G_FFN1, G_KV, G_ATTN = range(5)


def trunk(nc, x, pool_w, pool_rows, w_kv, w_q, w_o, w_gate, w_up, w_down, final_norm,
          gain_cols, sink_rows, bands, rope, out):
    def rows(w):
        return w.rearrange("(k p) n -> p k n", p=P)

    gate_v = [rows(w_gate[l]) for l in range(2)]
    up_v = [rows(w_up[l]) for l in range(2)]
    down_v = [rows(w_down[l]) for l in range(2)]
    kv_v, q_v, o_v = rows(w_kv), rows(w_q[0]), rows(w_o[0])
    pool_v = [rows(pool_w[0, g]) for g in range(NBLK)]
    x_v = x[0].rearrange("(t p) d -> p t d", p=P)
    out_v = out[0].rearrange("(t p) d -> p t d", p=P)

    with ExitStack() as ctx:
        top = [(nc.sbuf_base + 31) // 32 * 32]

        def at(name, shape, dt, offset):
            return nc.alloc_sbuf_tensor_at(name, shape, dt, offset=offset)

        def place(name, shape, dt):
            size = 4 * int(np.prod(shape[1:]))
            offset = top[0]
            top[0] += (size + 31) // 32 * 32
            return at(name, shape, dt, offset), offset

        h, _ = place("h", [P, T, D], F32)
        hT_hi, o_hi = place("hT_hi", [P, KF, S], F32R)
        hT_lo, o_lo = place("hT_lo", [P, KF, S], F32R)
        xT_hi, o_xhi = place("xT_hi", [P, KD, S], F32R)
        xT_lo, o_xlo = place("xT_lo", [P, KD, S], F32R)
        raw, _ = place("raw", [P, RING, 4 * C], F32)
        w_hi, _ = place("w_hi", [P, RING, 2 * C], F32R)
        w_lo, _ = place("w_lo", [P, RING, 2 * C], F32R)
        act, o_act = place("act", [P, T, C], F32)
        hblk = at("hblk", [P, T, C], F32, o_act)
        sqdump, _ = place("sqdump", [P, C], F32)
        ident, _ = place("ident", [P, P], F32)
        gains, _ = place("gains", [P, 5, KD], F32)
        sink, _ = place("sink", [P, GROUPS * PAIRS], F32)
        nsink, _ = place("nsink", [P, GROUPS * PAIRS], F32)
        ropes, _ = place("ropes", [P, 2, T, ROT], F32)
        sumsq, _ = place("sumsq", [P, T, NBLK], F32)
        total, _ = place("total", [P, T], F32)
        rms, _ = place("rms", [P, T], F32)
        r, _ = place("r", [P, T], F32)
        eps, _ = place("eps", [P, 1], F32)
        mx, _ = place("mx", [P, 2, PAIRS], F32)
        nmax, _ = place("nmax", [P, 2, PAIRS], F32)
        sinkd, _ = place("sinkd", [P, 2, PAIRS], F32)
        esink, _ = place("esink", [P, 2, PAIRS], F32)
        rsum, _ = place("rsum", [P, 2, PAIRS], F32)
        den, _ = place("den", [P, 2, PAIRS], F32)
        rden, _ = place("rden", [P, 2, PAIRS], F32)

        pT_hi, pT_lo = hT_hi[:, 0:KD, :], hT_lo[:, 0:KD, :]
        oT_hi, oT_lo = hT_hi[:, 0:KD, :], hT_lo[:, 0:KD, :]
        free_hi, free_lo = o_hi + 4 * KD * S, o_lo + 4 * KD * S
        xb = at("xb", [P, T, D], F32, free_hi)
        scale_b = at("scale_b", [P, D], F32, free_hi + 4 * T * D)
        bias_b = at("bias_b", [P, D], F32, free_lo)
        band = at("band", [P, len(WINDOWS), BANDW + P], F32, free_lo + 4 * D)
        band_r = at("band_r", [P, len(WINDOWS), BANDW + P], F32, free_lo + 4 * (D + 1088))
        vecs = at("vecs", [NBLK, 2, C], F32, o_hi)
        bprod = at("bprod", [NBLK, C], F32, o_hi + 4 * 2 * C)
        vec_r = at("vec_r", [NBLK, 2, 2, C], F32R, o_hi + 4 * 4 * C)
        pick = at("pick", [NBLK, NBLK, P], F32, free_lo + 4 * (D + 2 * 1088 + T * C))
        pick_r = at("pick_r", [NBLK, NBLK, P], F32R, free_lo + 4 * (D + 2 * 1088 + T * C + NBLK * P))
        top_ysc = free_lo + 4 * (D + 2 * 1088)
        ysc = at("ysc", [P, T, C], F32, free_lo + 4 * (D + 2 * 1088))
        kv = at("kv", [P, T, C], F32, free_hi)
        q = at("q", [P, T, C], F32, free_hi + 4 * 1024)
        rope_a = at("rope_a", [P, T, HPG, ROT], F32, free_hi + 4 * 2048)
        rope_b = at("rope_b", [P, T, HPG, ROT], F32, free_hi + 4 * 2304)
        kT = at("kT", [DH, GROUPS, 3, 2 * CHUNK], F32, free_hi + 4 * 2560)
        qT = at("qT", [DH, NCH, HPG, CHUNK], F32, free_hi + 4 * 4096)
        prob = at("prob", [P, 2, PAIRS, 2 * CHUNK], F32, free_lo)
        probT = at("probT", [P, 2, PAIRS, P], F32, free_lo + 4 * 1024)
        v_mid = at("v_mid", [P, GROUPS * DH], F32, free_lo + 4 * 2048)
        xsq0 = at("xsq0", [P, D], F32, o_xlo)
        xsq1 = at("xsq1", [P, D], F32, o_xhi)
        hsq = at("hsq", [P, T, C], F32, top_ysc)
        gfin = at("gfin", [P, D], F32, o_xlo)
        res = at("res", [P, T, D], F32, o_xhi)

        assert top[0] <= nc.sbuf_usable_end, top[0] - nc.sbuf_usable_end
        acc = ctx.enter_context(nc.psum_tensor("acc", [P, 8, C], F32))
        BIAS_BANK = (4, 5, 2, 3)
        TURN, WORK = 4, 6

        def sem(name):
            return ctx.enter_context(nc.semaphore(name))

        raw_in = [sem(f"raw_in{i}") for i in range(RING)]
        hi_ready = sem("hi_ready")
        unit_ready = sem("unit_ready")
        unit_used = sem("unit_used")
        job_out = sem("job_out")
        t_full = [sem(f"t_full{b}") for b in range(2)]
        t_hi = [sem(f"t_hi{b}") for b in range(2)]
        t_free = [sem(f"t_free{b}") for b in range(2)]
        sq_done = sem("sq_done")
        h_stored = sem("h_stored")
        total_ready = sem("total_ready")
        rms_ready = sem("rms_ready")
        r_ready = sem("r_ready")
        x_in = [sem(f"x_in{i}") for i in range(2 * T)]
        warm = sem("warm")
        pick_ready = sem("pick_ready")
        bprod_ready = sem("bprod_ready")
        vec_hi = sem("vec_hi")
        vec_lo = sem("vec_lo")
        spread = sem("spread")
        scale_ready = sem("scale_ready")
        bias_ready = sem("bias_ready")
        band_in, gains_in, small_in, scale_in, gfin_in = (sem(s) for s in (
            "band_in", "gains_in", "small_in", "scale_in", "gfin_in"))
        xsq_act = sem("xsq_act")
        xsq_dve = sem("xsq_dve")
        band_ready = sem("band_ready")
        ident_ready = sem("ident_ready")
        consts_ready = sem("consts_ready")
        xb_ready = sem("xb_ready")
        mix_full = sem("mix_full")
        mix_hi = sem("mix_hi")
        mix_free = sem("mix_free")
        ysc_done = sem("ysc_done")
        rope_step = sem("rope_step")
        kv_ready = sem("kv_ready")
        q_ready = sem("q_ready")
        s_full = sem("s_full")
        stat = sem("stat")
        sinkd_ready = sem("sinkd_ready")
        p_exp = sem("p_exp")
        den_step = sem("den_step")
        p_norm = sem("p_norm")
        tile0_done = sem("tile0_done")
        last_step = sem("last_step")
        res_ready = sem("res_ready")
        res_ready1 = sem("res_ready1")
        out_done = sem("out_done")

        def pair_bank(pair, t):
            return acc[:, bass.ds(2 * pair + t, 1), :].rearrange("p a n -> p (a n)")

        block = ctx.enter_context(nc.Block())

        @block.sync
        def _(sp):
            for t in range(T):
                for half in range(2):
                    cols = slice(half * D // 2, (half + 1) * D // 2)
                    sp.dma_start(h[:, t, cols], x_v[:, t, cols]).then_inc(x_in[2 * t + half], 16)
            sp.dma_start(band[:, :, :], bands).then_inc(band_in, 16)
            sp.dma_start(gains[:, :, :], gain_cols).then_inc(gains_in, 16)

            def load(lap, i, w, k0, tiles, col):
                ready = 8 * lap + 2 * i - 2 * RING + 2
                if not isinstance(ready, int) or ready > 0:
                    sp.wait_ge(unit_ready, ready)
                slot = i % RING
                sp.dma_start(raw[:, slot, 0:tiles * C].rearrange("p (k n) -> p k n", k=tiles),
                             w[:, k0:k0 + tiles, bass.ds(col, C)]).then_inc(raw_in[slot], 16)

            def load_gate_up(l, j):
                for m, w in enumerate((gate_v[l], up_v[l])):
                    for i, (k0, a, b) in enumerate(LOADS_D):
                        load(LAP_GU[l] + 2 * j, 4 * m + i, w, k0, a + b, j * C)

            def load_down(l, b):
                for i, (k0, a, c) in enumerate(LOADS_F):
                    load(LAP_DOWN[l] + 3 * b, i, down_v[l], k0, a + c, b * C)

            for g in range(NBLK):
                load(LAP_POOL, g, pool_v[g], 0, 4, 0)
                if g == 2:
                    sp.dma_start(sink[:, :], sink_rows).then_inc(small_in, 16)
                    sp.dma_start(ropes[:, :, :, :], rope).then_inc(small_in, 16)
            with sp.Fori(0, NFB) as j:
                load_gate_up(0, j)
            with sp.Fori(0, NBLK) as b:
                load_down(0, b)
            for i, (k0, a, c) in enumerate(LOADS_D):
                load(LAP_KV, i, kv_v, k0, a + c, 0)
            with sp.Fori(0, GROUPS) as g:
                for i, (k0, a, c) in enumerate(LOADS_D):
                    load(LAP_Q + g, i, q_v, k0, a + c, g * C)
            for n in range(0, 16, 2):
                job, i = O_FIRST[n]
                load(LAP_O, n // 2, o_v, 2 * i, 4, job * C)
            with sp.Fori(2, NBLK) as b:
                for i, (k0, a, c) in enumerate(LOADS_D):
                    load(LAP_O + b, i, o_v, k0, a + c, b * C)
            with sp.Fori(0, NFB) as j:
                load_gate_up(1, j)
            with sp.Fori(0, NBLK) as b:
                load_down(1, b)
            for t in range(T):
                sp.wait_ge(res_ready, t + 1)
                sp.dma_start(out_v[:, t, 0:D // 2], res[:, t, 0:D // 2]).then_inc(out_done, 16)
                sp.wait_ge(res_ready1, t + 1)
                sp.dma_start(out_v[:, t, D // 2:], res[:, t, D // 2:]).then_inc(out_done, 16)
            sp.wait_ge(out_done, 4 * 16)

        @block.scalar
        def _(ac):
            def round_hi(lap, i, tiles, off, gain=None, k0=0):
                if i % 2 == 0:
                    ac.wait_ge(raw_in[(i // 2) % RING], 16 * (lap + i // 8 + 1))
                used = 8 * lap + i - RING + 1
                if not isinstance(used, int) or used > 0:
                    ac.wait_ge(unit_used, used)
                slot = raw[:, (i // 2) % RING, off:off + tiles * C]
                if gain is None:
                    nc.scalar.activation(w_hi[:, i % RING, 0:tiles * C], slot, ACT.Copy).then_inc(hi_ready, 1)
                    return
                for kk in range(tiles):
                    last = nc.scalar.activation(w_hi[:, i % RING, kk * C:(kk + 1) * C],
                                                slot[:, kk * C:(kk + 1) * C], ACT.Copy,
                                                scale=gains[:, gain, k0 + kk:k0 + kk + 1])
                last.then_inc(hi_ready, 1)

            def turn_hi(fill, dst, k, gain=None):
                for b in range(2):
                    ac.wait_ge(t_full[b], fill + 1)
                    if gain is None:
                        last = nc.scalar.activation(
                            dst[:, bass.ds(k + 2 * b, 2), :],
                            acc[:, TURN + b, :].rearrange("p (a s) -> p a s", a=2), ACT.Copy)
                    else:
                        for a in range(2):
                            kk = k + 2 * b + a
                            last = nc.scalar.activation(dst[:, kk, :], acc[:, TURN + b, a * S:(a + 1) * S],
                                                        ACT.Copy, scale=gains[:, gain, kk:kk + 1])
                    last.then_inc(t_hi[b], 1)

            def mix_hi_part(g):
                for b in range(2):
                    ac.wait_ge(mix_full, 2 * g + b + 1)
                    for a in range(2):
                        kk = 4 * g + 2 * b + a
                        last = nc.scalar.activation(pT_hi[:, kk, :], acc[:, WORK + b, a * S:(a + 1) * S],
                                                    ACT.Copy, scale=gains[:, G_POOL, kk:kk + 1])
                    last.then_inc(mix_hi, 1)

            def squares(job, c, blk):
                ac.wait_ge(job_out, job + 1)
                for t in range(T):
                    if not isinstance(blk, int) or blk + t > 0:
                        ac.wait_ge(sq_done, 2 * blk + t)
                    else:
                        ac.wait_ge(warm, 1)
                    nc.scalar.activation(sqdump[:, :], hblk[:, t, :], ACT.Square,
                                         accum_out=sumsq[:, t, bass.ds(c, 1)]).then_inc(sq_done, 1)

            def root(n, t=None):
                cols = slice(0, T) if t is None else slice(t, t + 1)
                ac.wait_ge(total_ready, n + 1)
                nc.scalar.activation(rms[:, cols], total[:, cols], ACT.Sqrt, bias=eps[:, :],
                                     scale=1.0 / D).then_inc(rms_ready, 1)

            def gate_out(l, j):
                job = JOB_GU[l] + 2 * j
                ac.wait_ge(unit_used, 8 * (LAP_GU[l] + 2 * j) + UD)
                if isinstance(j, int):
                    ac.wait_ge(r_ready, 2 + 2 * l)
                    ac.wait_ge(h_stored, [4, 12][l])
                for t in range(T):
                    last = nc.scalar.activation(act[:, t, :], acc[:, 2 * (JOB_GU[l] % 2) + t, :], ACT.Silu,
                                                scale=r[:, t:t + 1])
                last.then_inc(job_out, 1)

            nc.scalar.dma_start(vecs[:, :, :], pool_rows).then_inc(scale_in, 16)
            ac.wait_ge(consts_ready, 1)
            nc.scalar.activation(sqdump[:, 0:1], eps[:, :], ACT.Sqrt).then_inc(warm, 1)
            ac.wait_ge(ident_ready, 2)
            nc.scalar.activation(pick_r[:, :, :], pick[:, :, :], ACT.Copy).then_inc(pick_ready, 1)
            ac.wait_ge(scale_in, 16)
            nc.scalar.activation(vec_r[:, 0, 0, :], vecs[:, 0, :], ACT.Copy).then_inc(vec_hi, 1)
            ac.wait_ge(bprod_ready, 1)
            nc.scalar.activation(vec_r[:, 1, 0, :], bprod[:, :], ACT.Copy).then_inc(vec_hi, 1)
            for t in range(T):
                ac.wait_ge(x_in[2 * t], 16)
                nc.scalar.activation(xsq0[:, t * D // 2:(t + 1) * D // 2], h[:, t, 0:D // 2], ACT.Square,
                                     accum_out=sumsq[:, t, 0:1]).then_inc(xsq_act, 1)
            root(0)
            for c in range(NBLK):
                ac.wait_ge(spread, c + 1)
                nc.scalar.activation(scale_b[:, c * C:(c + 1) * C], acc[:, c, :], ACT.Copy).then_inc(scale_ready, 1)

            def bias_out(c):
                ac.wait_ge(spread, NBLK + c + 1)
                nc.scalar.activation(bias_b[:, c * C:(c + 1) * C], acc[:, BIAS_BANK[c], :],
                                     ACT.Copy).then_inc(bias_ready, 1)

            ac.wait_ge(gains_in, 16)
            for i in range(8):
                round_hi(LAP_POOL, i, 2, (i % 2) * 2 * C)
                if i == 1:
                    mix_hi_part(0)
                    for c in range(NBLK):
                        bias_out(c)
                    mix_hi_part(1)
                if i == 5:
                    mix_hi_part(2)
            turn_hi(FILL_POOL, xT_hi, 0, G_FFN0)
            mix_hi_part(3)
            squares(0, 0, 0)

            def gate_up(l, j, first):
                lap = LAP_GU[l] + 2 * j
                for i in range(2 * UD):
                    k0, tiles, off = UNITS_D[i % UD]
                    round_hi(lap, i, tiles, off)
                    if first and l == 0:
                        if i == 1 or i == 3:
                            c = i // 2 + 1
                            turn_hi(FILL_POOL + c, xT_hi, 4 * c, G_FFN0)
                            squares(c, c, c)
                        if i == 5:
                            turn_hi(FILL_POOL + 3, xT_hi, 12, G_FFN0)
                            squares(3, 3, 3)
                    if first and l == 1 and i == 5:
                        turn_hi(FILL_O + 3, xT_hi, 12, G_FFN1)
                        squares(JOB_O + 3, 3, BLK_O + 3)
                    if first and i == 7:
                        root(1 + 2 * l)
                    if not first and i == 5:
                        turn_hi(FILL_ACT[l] + j - 1, hT_hi, 4 * j - 4)
                    if i == 10:
                        gate_out(l, j)

            def down(l, b, first):
                lap = LAP_DOWN[l] + 3 * b
                for i, (k0, tiles, off) in enumerate(UNITS_F):
                    round_hi(lap, i, tiles, off)
                    if first and i == 5:
                        turn_hi(FILL_ACT[l] + NFB - 1, hT_hi, 4 * NFB - 4)
                        if l == 1:
                            nc.scalar.dma_start(gfin[:, :], final_norm.partition_broadcast(P)).then_inc(gfin_in, 16)
                    if not first and i == 5:
                        if l == 0:
                            turn_hi(FILL_DOWN + b - 1, xT_hi, 4 * b - 4)
                        squares(JOB_DOWN[l] + b - 1, b - 1, BLK_DOWN[l] + b - 1)

            gate_up(0, 0, True)
            with ac.Fori(1, NFB) as j:
                gate_up(0, j, False)
            down(0, 0, True)
            with ac.Fori(1, NBLK) as b:
                down(0, b, False)

            def exps(item):
                g, n = item // NCH, item % NCH
                keys = CHUNK if n == 0 else 2 * CHUNK
                e = n % 2
                ac.wait_ge(sinkd_ready, item + 1)
                if item >= 2:
                    before, half = (item - 2) // NCH, ((item - 2) % NCH) // 2
                    ac.wait_ge(t_full[e], FILL_G + 6 * before + 2 + 2 * half + 1)
                nc.scalar.activation(esink[:, e, :], sinkd[:, e, :], ACT.Exp)
                for j in range(PAIRS):
                    last = nc.scalar.activation(prob[:, e, j, 0:keys],
                                                acc[:, WORK + e, j * P:j * P + keys], ACT.Exp,
                                                bias=nmax[:, e, j:j + 1], scale=SCALE,
                                                accum_out=rsum[:, e, j:j + 1])
                last.then_inc(p_exp, 1)

            def q_out(job, dst):
                pair = job % 2
                for t in range(T):
                    last = nc.scalar.activation(dst[:, t, :], acc[:, 2 * pair + t, :], ACT.Copy,
                                                scale=r[:, t:t + 1])
                last.then_inc(job_out, 1)

            def q_turn(g, t):
                ac.wait_ge(t_full[0], FILL_G + 6 * g + t + 1)
                nc.scalar.activation(
                    qT[:, 2 * t:2 * t + 2, 0:4, :].rearrange("d n h s -> d h n s"),
                    acc[0:DH, TURN, :].rearrange("d (h n s) -> d h n s", h=4, n=2),
                    ACT.Copy).then_inc(t_free[0], 1)

            def prob_turn(g, half):
                keys = CHUNK if half == 0 else P
                ac.wait_ge(t_full[0], FILL_G + 6 * g + 2 + 2 * half + 1)
                nc.scalar.activation(probT[0:keys, 0, :, :].rearrange("k a s -> k (a s)"),
                                     acc[0:keys, TURN, :], ACT.Copy).then_inc(t_free[0], 1)

            def o_hi_part(g, half):
                for e in range(2):
                    n = 2 * half + e
                    ac.wait_ge(t_full[e], FILL_G + 6 * g + 3 + 2 * half + 1)
                    nc.scalar.activation(oT_hi[:, PAIRS * g:PAIRS * (g + 1), n * CHUNK:(n + 1) * CHUNK],
                                         acc[:, TURN + e, 0:PAIRS * CHUNK].rearrange("p (a s) -> p a s", a=PAIRS),
                                         ACT.Copy).then_inc(t_hi[e], 1)

            def attention_step(g, s):
                if s == 2:
                    q_turn(g, 0)
                if s == 3:
                    q_turn(g, 1)
                if s == 4:
                    exps(NCH * g)
                if s == 5:
                    exps(NCH * g + 1)
                if s == 6:
                    prob_turn(g, 0)
                    exps(NCH * g + 2)
                if s == 7:
                    o_hi_part(g, 0)
                    exps(NCH * g + 3)
                if s == 8:
                    prob_turn(g, 1)
                if s == 9:
                    o_hi_part(g, 1)

            for i, (k0, tiles, off) in enumerate(UNITS_D):
                round_hi(LAP_KV, i, tiles, off, G_KV, k0)
                if i == 5:
                    turn_hi(FILL_DOWN + 3, xT_hi, 12)
                    squares(JOB_DOWN[0] + 3, 3, BLK_DOWN[0] + 3)
                if i == 7:
                    root(2)
            for g in range(GROUPS):
                for i, (k0, tiles, off) in enumerate(UNITS_D):
                    round_hi(LAP_Q + g, i, tiles, off, G_ATTN, k0)
                    if i == 2:
                        ac.wait_ge(unit_used, 8 * (LAP_Q + g))
                        if g == 0:
                            ac.wait_ge(r_ready, 3)
                            for half, t in ((0, 1), (1, 0)):
                                tok = slice(half * CHUNK, (half + 1) * CHUNK)
                                nc.scalar.activation(v_mid[tok, :], acc[tok, 2 * (JOB_KV % 2) + t, GROUPS * DH:],
                                                     ACT.Copy, scale=r[tok, t:t + 1])
                            q_out(JOB_KV, kv)
                        else:
                            if g >= 2:
                                ac.wait_ge(t_full[1], FILL_G + 6 * (g - 2) + 2)
                            q_out(JOB_Q + g - 1, q)
                    if g == 0 and i == 6:
                        ac.wait_ge(t_full[0], FILL_K + 1)
                        kT0 = acc[0:DH, TURN, :].rearrange("d (g s) -> d g s", g=GROUPS)
                        nc.scalar.activation(kT[:, :, 0, :], kT0, ACT.Copy)
                        nc.scalar.activation(kT[:, :, 1, CHUNK:], kT0[:, :, CHUNK:], ACT.Copy).then_inc(t_free[0], 1)
                    if g >= 2 and i < 5:
                        attention_step(g - 2, i + 5)
                    if g >= 1 and i >= 5:
                        attention_step(g - 1, i - 3)
            for n, (job, i) in enumerate(O_FIRST):
                k0, tiles, off = UNITS_D[i]
                round_hi(LAP_O, n, tiles, (n % 2) * 2 * C)
                if n == 2:
                    ac.wait_ge(unit_used, 8 * LAP_O)
                    ac.wait_ge(t_full[1], FILL_G + 6 * 2 + 2)
                    q_out(JOB_Q + 3, q)
                if n < 5:
                    attention_step(2, n + 5)
                if n >= 5:
                    attention_step(3, n - 3)
            for b in range(2, NBLK):
                for i, (k0, tiles, off) in enumerate(UNITS_D):
                    round_hi(LAP_O + b, i, tiles, off)
                    c = {(2, 3): 0, (2, 6): 1, (3, 5): 2}.get((b, i))
                    if c is not None:
                        turn_hi(FILL_O + c, xT_hi, 4 * c, G_FFN1)
                        squares(JOB_O + c, c, BLK_O + c)

            gate_up(1, 0, True)
            with ac.Fori(1, NFB) as j:
                gate_up(1, j, False)
            ac.wait_ge(sq_done, 2 * BLK_DOWN[1])
            nc.scalar.activation(sqdump[:, 0:1], eps[:, :], ACT.Sqrt).then_inc(warm, 1)
            ac.wait_ge(warm, 2)
            down(1, 0, True)
            with ac.Fori(1, NBLK) as b:
                down(1, b, False)
            ac.wait_ge(h_stored, 4 * NBLK - 1)
            for t in range(T):
                root(4 + t, t)
                ac.wait_ge(r_ready, 5 + t)
                nc.scalar.activation(res[:, t, 0:2 * C], h[:, t, 0:2 * C], ACT.Copy,
                                     scale=r[:, t:t + 1]).then_inc(res_ready, 1)

        @block.vector
        def _(ve):
            def split_lo(lap, i, tiles, off, gain=None, k0=0):
                ve.wait_ge(hi_ready, 8 * lap + i + 1)
                slot = raw[:, (i // 2) % RING, off:off + tiles * C]
                if gain is None:
                    nc.vector.tensor_tensor(w_lo[:, i % RING, 0:tiles * C], slot,
                                            w_hi[:, i % RING, 0:tiles * C].bitcast(F32),
                                            ALU.subtract).then_inc(unit_ready, 1)
                    return
                for kk in range(tiles):
                    last = nc.vector.scalar_tensor_tensor(
                        out=w_lo[:, i % RING, kk * C:(kk + 1) * C], in0=slot[:, kk * C:(kk + 1) * C],
                        scalar=gains[:, gain, k0 + kk:k0 + kk + 1],
                        in1=w_hi[:, i % RING, kk * C:(kk + 1) * C].bitcast(F32), op0=ALU.mult, op1=ALU.subtract)
                last.then_inc(unit_ready, 1)

            def lo_of(dst, hi, src, gain, k):
                return nc.vector.scalar_tensor_tensor(out=dst[:, k, :], in0=src, scalar=gains[:, gain, k:k + 1],
                                                      in1=hi[:, k, :].bitcast(F32), op0=ALU.mult,
                                                      op1=ALU.subtract)

            def turn_lo(fill_hi, dst, hi, k, gain=None):
                for b in range(2):
                    ve.wait_ge(t_hi[b], fill_hi + 1)
                    if gain is None:
                        last = nc.vector.tensor_tensor(
                            dst[:, bass.ds(k + 2 * b, 2), :],
                            acc[:, TURN + b, :].rearrange("p (a s) -> p a s", a=2),
                            hi[:, bass.ds(k + 2 * b, 2), :].bitcast(F32), ALU.subtract)
                    else:
                        for a in range(2):
                            last = lo_of(dst, hi, acc[:, TURN + b, a * S:(a + 1) * S], gain, k + 2 * b + a)
                    last.then_inc(t_free[b], 1)

            def mix_lo_part(g):
                for b in range(2):
                    ve.wait_ge(mix_hi, 2 * g + b + 1)
                    for a in range(2):
                        last = lo_of(pT_lo, pT_hi, acc[:, WORK + b, a * S:(a + 1) * S], G_POOL, 4 * g + 2 * b + a)
                    last.then_inc(mix_free, 1)

            def pool_out(g):
                ve.wait_ge(unit_used, 2 * g + 2)
                ve.wait_ge(xb_ready, g + 1)
                if g > 0:
                    hblk_free(g, FILL_POOL + g - 1)
                for t in range(T):
                    nc.vector.tensor_tensor(ysc[:, t, :], acc[:, 2 * (g % 2) + t, :],
                                            scale_b[:, g * C:(g + 1) * C], ALU.mult).then_inc(ysc_done, 1)
                for t in range(T):
                    ve.wait_ge(ysc_done, 2 * g + t + 1)
                    last = nc.vector.tensor_tensor(hblk[:, t, :], ysc[:, t, :], xb[:, t, g * C:(g + 1) * C],
                                                   ALU.add)
                last.then_inc(job_out, 1)

            def hblk_free(blk, fill):
                if fill is not None:
                    ve.wait_ge(t_full[1], fill + 1)
                ve.wait_ge(sq_done, 2 * blk)
                ve.wait_ge(h_stored, blk)

            def residual_out(pair, c, used, blk, fill):
                ve.wait_ge(unit_used, used)
                hblk_free(blk, fill)
                for t in range(T):
                    last = nc.vector.tensor_tensor(hblk[:, t, :], pair_bank(pair, t), h[:, t, bass.ds(c * C, C)],
                                                   ALU.add)
                last.then_inc(job_out, 1)

            def sum_up(blk):
                ve.wait_ge(sq_done, 2 * blk + 2)
                nc.vector.reduce_sum(total[:, :], sumsq[:, :, :], AX_X).then_inc(total_ready, 1)

            def invert(n):
                ve.wait_ge(rms_ready, n + 1)
                nc.vector.reciprocal(r[:, :], rms[:, :]).then_inc(r_ready, 1)

            def up_out(l, j):
                job = JOB_GU[l] + 2 * j + 1
                pair = (JOB_GU[l] + 1) % 2
                ve.wait_ge(unit_used, 8 * (LAP_GU[l] + 2 * j) + 2 * UD)
                ve.wait_ge(job_out, job)
                for t in range(T):
                    last = nc.vector.scalar_tensor_tensor(out=act[:, t, :], in0=acc[:, 2 * pair + t, :],
                                                          scalar=r[:, t:t + 1], in1=act[:, t, :],
                                                          op0=ALU.mult, op1=ALU.mult)
                last.then_inc(job_out, 1)

            nc.vector.memset(eps[:, :], EPS).then_inc(consts_ready, 1)
            ve.wait_ge(scale_in, 16)
            nc.vector.tensor_tensor(bprod[:, :], vecs[:, 1, :], vecs[:, 0, :], ALU.mult).then_inc(bprod_ready, 1)
            ve.wait_ge(vec_hi, 1)
            nc.vector.tensor_tensor(vec_r[:, 0, 1, :], vecs[:, 0, :], vec_r[:, 0, 0, :].bitcast(F32),
                                    ALU.subtract).then_inc(vec_lo, 1)
            ve.wait_ge(vec_hi, 2)
            ve.wait_ge(bprod_ready, 1)
            nc.vector.tensor_tensor(vec_r[:, 1, 1, :], bprod[:, :], vec_r[:, 1, 0, :].bitcast(F32),
                                    ALU.subtract).then_inc(vec_lo, 1)
            for t in range(T):
                ve.wait_ge(x_in[2 * t + 1], 16)
                nc.vector.scalar_tensor_tensor(out=xsq1[:, t * D // 2:(t + 1) * D // 2], in0=h[:, t, D // 2:],
                                               scalar=1.0, in1=h[:, t, D // 2:], op0=ALU.mult, op1=ALU.mult,
                                               accum_out=sumsq[:, t, 1:2]).then_inc(xsq_dve, 1)
            ve.wait_ge(xsq_act, 2)
            ve.wait_ge(xsq_dve, 2)
            nc.vector.tensor_tensor(total[:, :], sumsq[:, :, 0], sumsq[:, :, 1], ALU.add).then_inc(total_ready, 1)
            invert(0)
            ve.wait_ge(band_in, 16)
            ve.wait_ge(r_ready, 1)
            nc.vector.tensor_scalar(band_r[:, :, 0:BANDW], band[:, :, 0:BANDW], r[:, 0:1], None, ALU.mult)
            nc.vector.tensor_scalar(band_r[:, :, BANDW:], band[:, :, BANDW:], r[:, 1:2], None,
                                    ALU.mult).then_inc(band_ready, 1)
            ve.wait_ge(gains_in, 16)
            for i in range(8):
                split_lo(LAP_POOL, i, 2, (i % 2) * 2 * C)
                if i == 1:
                    mix_lo_part(0)
                    mix_lo_part(1)
                if i == 5:
                    pool_out(0)
                    mix_lo_part(2)
            turn_lo(HI_POOL, xT_lo, xT_hi, 0, G_FFN0)
            mix_lo_part(3)
            pool_out(1)

            def gate_up(l, j, first):
                lap = LAP_GU[l] + 2 * j
                for i in range(2 * UD):
                    k0, tiles, off = UNITS_D[i % UD]
                    split_lo(lap, i, tiles, off)
                    if first and l == 0:
                        if i == 1 or i == 3:
                            c = i // 2 + 1
                            turn_lo(HI_POOL + c, xT_lo, xT_hi, 4 * c, G_FFN0)
                            pool_out(c + 1)
                        if i == 5:
                            turn_lo(HI_POOL + 3, xT_lo, xT_hi, 12, G_FFN0)
                    if first and l == 1:
                        if i == 2:
                            residual_out((JOB_O + 3) % 2, 3, 8 * LAP_GU[1], BLK_O + 3, FILL_O + 2)
                        if i == 5:
                            turn_lo(HI_O + 3, xT_lo, xT_hi, 12, G_FFN1)
                    if first and i == 6:
                        sum_up(3 if l == 0 else BLK_O + 3)
                    if first and i == 8:
                        invert(1 + 2 * l)
                        ve.wait_ge(r_ready, 2 + 2 * l)
                    if not first and i == 2:
                        up_out(l, j - 1)
                    if not first and i == 5:
                        turn_lo(HI_ACT[l] + j - 1, hT_lo, hT_hi, 4 * j - 4)

            def down(l, b, first):
                lap = LAP_DOWN[l] + 3 * b
                for i, (k0, tiles, off) in enumerate(UNITS_F):
                    split_lo(lap, i, tiles, off)
                    if first and i == 2:
                        up_out(l, NFB - 1)
                    if first and i == 5:
                        turn_lo(HI_ACT[l] + NFB - 1, hT_lo, hT_hi, 4 * NFB - 4)
                    if not first and i == 2:
                        pair = (JOB_DOWN[l] + b - 1) % 2
                        residual_out(pair, b - 1, 8 * lap, BLK_DOWN[l] + b - 1,
                                     FILL_DOWN + b - 2 if l == 0 else None)
                    if not first and i == 5 and l == 0:
                        turn_lo(HI_DOWN + b - 1, xT_lo, xT_hi, 4 * b - 4)

            gate_up(0, 0, True)
            with ve.Fori(1, NFB) as j:
                gate_up(0, j, False)
            down(0, 0, True)
            with ve.Fori(1, NBLK) as b:
                down(0, b, False)

            def row_stats(item):
                g, n = item // NCH, item % NCH
                keys = CHUNK if n == 0 else 2 * CHUNK
                e = n % 2
                heads = slice(PAIRS * g, PAIRS * (g + 1))
                ve.wait_ge(s_full, item + 1)
                nc.vector.reduce_max(mx[:, e, :], acc[:, WORK + e, :].rearrange("p (a k) -> p a k", a=PAIRS)[:, :, 0:keys],
                                     AX_X).then_inc(stat, 1)
                ve.wait_ge(stat, 2 * item + 1)
                nc.vector.scalar_tensor_tensor(out=nmax[:, e, :], in0=mx[:, e, :], scalar=-SCALE,
                                               in1=nsink[:, heads], op0=ALU.mult, op1=ALU.min).then_inc(stat, 1)
                ve.wait_ge(stat, 2 * item + 2)
                nc.vector.tensor_tensor(sinkd[:, e, :], sink[:, heads], nmax[:, e, :],
                                        ALU.add).then_inc(sinkd_ready, 1)

            def normalise(item):
                n = item % NCH
                keys = CHUNK if n == 0 else 2 * CHUNK
                e = n % 2
                ve.wait_ge(p_exp, item + 1)
                nc.vector.tensor_tensor(den[:, e, :], rsum[:, e, :], esink[:, e, :], ALU.add).then_inc(den_step, 1)
                ve.wait_ge(den_step, 2 * item + 1)
                nc.vector.reciprocal(rden[:, e, :], den[:, e, :]).then_inc(den_step, 1)
                ve.wait_ge(den_step, 2 * item + 2)
                nc.vector.tensor_tensor(prob[:, e, :, 0:keys], prob[:, e, :, 0:keys],
                                        rden[:, e, :].unsqueeze(2).to_broadcast([P, PAIRS, keys]),
                                        ALU.mult).then_inc(p_norm, 1)

            def q_turn(g, t):
                ve.wait_ge(t_full[1], FILL_G + 6 * g + t + 1)
                nc.vector.tensor_copy(
                    qT[:, 2 * t:2 * t + 2, 4:8, :].rearrange("d n h s -> d h n s"),
                    acc[0:DH, TURN + 1, :].rearrange("d (h n s) -> d h n s", h=4, n=2)).then_inc(t_free[1], 1)

            def prob_turn(g, half):
                ve.wait_ge(t_full[1], FILL_G + 6 * g + 2 + 2 * half + 1)
                nc.vector.tensor_copy(probT[:, 1, :, :].rearrange("k a s -> k (a s)"),
                                      acc[:, TURN + 1, :]).then_inc(t_free[1], 1)

            def o_lo_part(g, half):
                for e in range(2):
                    n = 2 * half + e
                    ve.wait_ge(t_hi[e], HI_G + 2 * g + half + 1)
                    cols = slice(n * CHUNK, (n + 1) * CHUNK)
                    nc.vector.tensor_tensor(oT_lo[:, PAIRS * g:PAIRS * (g + 1), cols],
                                            acc[:, TURN + e, 0:PAIRS * CHUNK].rearrange("p (a s) -> p a s", a=PAIRS),
                                            oT_hi[:, PAIRS * g:PAIRS * (g + 1), cols].bitcast(F32),
                                            ALU.subtract).then_inc(t_free[e], 1)

            def attention_step(g, s):
                if s == 2:
                    q_turn(g, 0)
                if s == 3:
                    q_turn(g, 1)
                if s == 4:
                    row_stats(NCH * g)
                    row_stats(NCH * g + 1)
                if s == 5:
                    normalise(NCH * g)
                    row_stats(NCH * g + 2)
                    normalise(NCH * g + 1)
                if s == 6:
                    prob_turn(g, 0)
                    row_stats(NCH * g + 3)
                    normalise(NCH * g + 2)
                if s == 7:
                    o_lo_part(g, 0)
                    normalise(NCH * g + 3)
                if s == 8:
                    prob_turn(g, 1)
                if s == 9:
                    o_lo_part(g, 1)

            for i, (k0, tiles, off) in enumerate(UNITS_D):
                split_lo(LAP_KV, i, tiles, off, G_KV, k0)
                if i == 2:
                    residual_out((JOB_DOWN[0] + 3) % 2, 3, 8 * LAP_KV, BLK_DOWN[0] + 3, FILL_DOWN + 2)
                if i == 5:
                    turn_lo(HI_DOWN + 3, xT_lo, xT_hi, 12)
                if i == 6:
                    sum_up(BLK_DOWN[0] + 3)
            for g in range(GROUPS):
                for i, (k0, tiles, off) in enumerate(UNITS_D):
                    split_lo(LAP_Q + g, i, tiles, off, G_ATTN, k0)
                    if g == 0 and i == 0:
                        invert(2)
                    if g == 0 and i == 6:
                        ve.wait_ge(t_full[1], FILL_K + 1)
                        kT1 = acc[0:DH, TURN + 1, :].rearrange("d (g s) -> d g s", g=GROUPS)
                        nc.vector.tensor_copy(kT[:, :, 2, :], kT1)
                        nc.vector.tensor_copy(kT[:, :, 1, 0:CHUNK], kT1[:, :, 0:CHUNK]).then_inc(t_free[1], 1)
                    if g >= 2 and i < 5:
                        attention_step(g - 2, i + 5)
                    if g >= 1 and i >= 5:
                        attention_step(g - 1, i - 3)
            for n, (job, i) in enumerate(O_FIRST):
                k0, tiles, off = UNITS_D[i]
                split_lo(LAP_O, n, tiles, (n % 2) * 2 * C)
                if n < 5:
                    attention_step(2, n + 5)
                if n >= 5:
                    attention_step(3, n - 3)
            for b in range(2, NBLK):
                for i, (k0, tiles, off) in enumerate(UNITS_D):
                    split_lo(LAP_O + b, i, tiles, off)
                    c = {(2, 3): 0, (2, 6): 1, (3, 5): 2}.get((b, i))
                    if c is not None:
                        turn_lo(HI_O + c, xT_lo, xT_hi, 4 * c, G_FFN1)
                    if b == 2 and i == 0:
                        residual_out(JOB_O % 2, 0, 8 * LAP_O + 14, BLK_O, FILL_DOWN + 3)
                    if b == 2 and i == 3:
                        residual_out((JOB_O + 1) % 2, 1, 8 * LAP_O + 16, BLK_O + 1, FILL_O)
                    if b == 3 and i == 2:
                        residual_out((JOB_O + 2) % 2, 2, 8 * (LAP_O + 3), BLK_O + 2, FILL_O + 1)
            gate_up(1, 0, True)
            with ve.Fori(1, NFB) as j:
                gate_up(1, j, False)
            down(1, 0, True)
            with ve.Fori(1, NBLK) as b:
                down(1, b, False)
            hblk_free(BLK_DOWN[1] + 3, None)
            for t in range(T):
                if t == 0:
                    ve.wait_ge(tile0_done, 1)
                else:
                    ve.wait_ge(unit_used, 8 * LAP_DOWN[1] + NBLK * UF)
                nc.vector.tensor_tensor(hblk[:, t, :], pair_bank((JOB_DOWN[1] + 3) % 2, t),
                                        h[:, t, 3 * C:], ALU.add).then_inc(last_step, 1)
                ve.wait_ge(last_step, 3 * t + 1)
                nc.vector.scalar_tensor_tensor(out=hsq[:, t, :], in0=hblk[:, t, :], scalar=1.0, in1=hblk[:, t, :],
                                               op0=ALU.mult, op1=ALU.mult,
                                               accum_out=sumsq[:, t, NBLK - 1:NBLK]).then_inc(last_step, 1)
                ve.wait_ge(last_step, 3 * t + 2)
                nc.vector.reduce_sum(total[:, t:t + 1], sumsq[:, t, :], AX_X).then_inc(total_ready, 1)
                nc.vector.tensor_tensor(hblk[:, t, :], hblk[:, t, :], gfin[:, 3 * C:], ALU.mult).then_inc(last_step, 1)
                ve.wait_ge(rms_ready, 5 + t)
                nc.vector.reciprocal(r[:, t:t + 1], rms[:, t:t + 1]).then_inc(r_ready, 1)
                ve.wait_ge(r_ready, 5 + t)
                ve.wait_ge(last_step, 3 * t + 3)
                nc.vector.tensor_scalar(res[:, t, 3 * C:], hblk[:, t, :], r[:, t:t + 1], None, ALU.mult)
                nc.vector.tensor_scalar(res[:, t, 2 * C:3 * C], h[:, t, 2 * C:3 * C], r[:, t:t + 1], None,
                                        ALU.mult).then_inc(res_ready1, 1)

        @block.tensor
        def _(te):
            def product(lap, i, at_hi, at_lo, k0, tiles, pair, first, last_unit, tokens=range(T)):
                te.wait_ge(unit_ready, 8 * lap + i + 1)
                w = i % RING
                for kk in range(tiles):
                    k = k0 + kk
                    cols = slice(kk * C, (kk + 1) * C)
                    for t in tokens:
                        tok = slice(t * P, (t + 1) * P)
                        dst = pair_bank(pair, t)
                        end = last_unit and kk == tiles - 1
                        nc.tensor.matmul(dst, at_hi[:, k, tok], w_hi[:, w, cols], start=first and kk == 0, stop=False)
                        nc.tensor.matmul(dst, at_hi[:, k, tok], w_lo[:, w, cols], start=False, stop=False)
                        last = nc.tensor.matmul(dst, at_lo[:, k, tok], w_hi[:, w, cols], start=False, stop=end)
                if T - 1 in tokens:
                    last.then_inc(unit_used, 1)
                return last

            def pair_free(job):
                if not isinstance(job, int) or job >= 2:
                    te.wait_ge(job_out, job - 1)

            def turn(src, fill):
                for b in range(2):
                    if not isinstance(fill, int) or fill > 0:
                        te.wait_ge(t_free[b], fill)
                    for a in range(2):
                        for t in range(T):
                            last = nc.tensor.transpose(acc[:, TURN + b, a * S + t * P:a * S + (t + 1) * P],
                                                       src[:, t, (2 * b + a) * P:(2 * b + a + 1) * P], ident[:, :])
                    last.then_inc(t_full[b], 1)

            def mix(g):
                for b in range(2):
                    if g > 0:
                        te.wait_ge(mix_free, 2 * g - 1 + b)
                    for a in range(2):
                        feats = slice((4 * g + 2 * b + a) * P, (4 * g + 2 * b + a + 1) * P)
                        nc.tensor.matmul(acc[:, WORK + b, a * S:a * S + BANDW], h[:, 0, feats],
                                         band_r[:, g, 0:BANDW], start=True, stop=False, skip_group_check=True)
                        last = nc.tensor.matmul(acc[:, WORK + b, a * S + P:(a + 1) * S], h[:, 1, feats],
                                                band_r[:, g, BANDW:], start=False, stop=True, skip_group_check=True)
                    last.then_inc(mix_full, 1)

            def pool_job(g):
                pair_free(g)
                te.wait_ge(mix_free, 2 * g + 2)
                for u in range(2):
                    product(LAP_POOL, 2 * g + u, pT_hi, pT_lo, 4 * g + 2 * u, 2, g % 2, u == 0, u == 1)

            def spread_block(v, c, bank):
                for part in range(2):
                    last = nc.tensor.matmul(acc[:, bank, :], pick_r[:, c, :], vec_r[:, v, part, :],
                                            start=part == 0, stop=part == 1)
                last.then_inc(spread, 1)

            te.wait_ge(pick_ready, 1)
            te.wait_ge(vec_lo, 1)
            for c in range(NBLK):
                spread_block(0, c, c)
            te.wait_ge(vec_lo, 2)
            spread_block(1, 0, BIAS_BANK[0])
            spread_block(1, 1, BIAS_BANK[1])
            te.wait_ge(band_ready, 1)
            mix(0)
            te.wait_ge(scale_ready, NBLK)
            spread_block(1, 2, BIAS_BANK[2])
            spread_block(1, 3, BIAS_BANK[3])
            mix(1)
            pool_job(0)
            mix(2)
            te.wait_ge(bias_ready, NBLK)
            pool_job(1)
            te.wait_ge(ident_ready, 4)
            te.wait_ge(job_out, 1)
            turn(hblk, FILL_POOL)
            mix(3)
            pool_job(2)
            te.wait_ge(job_out, 2)
            turn(hblk, FILL_POOL + 1)
            pool_job(3)
            te.wait_ge(job_out, 3)
            turn(hblk, FILL_POOL + 2)

            def gate_up(l, j, first):
                lap = LAP_GU[l] + 2 * j
                for m in range(2):
                    job = JOB_GU[l] + 2 * j + m
                    pair_free(job)
                    for u, (k0, tiles, _) in enumerate(UNITS_D):
                        if first and m == 0 and u % 2 == 0:
                            te.wait_ge(t_free[1], [FILL_POOL, FILL_O][l] + u // 2 + 1)
                        product(lap, UD * m + u, xT_hi, xT_lo, k0, tiles, (JOB_GU[l] + m) % 2, u == 0, u == UD - 1)
                        if m == 0 and u == 2:
                            te.wait_ge(job_out, JOB_GU[l] + 2 * j)
                            if first:
                                turn(hblk, [FILL_POOL, FILL_O][l] + 3)
                            else:
                                turn(act, FILL_ACT[l] + j - 1)

            def down(l, b, first):
                job = JOB_DOWN[l] + b
                pair_free(job)
                if first:
                    te.wait_ge(t_free[1], FILL_ACT[l] + NFB - 1)
                for u, (k0, tiles, _) in enumerate(UNITS_F):
                    if first and k0 + tiles > KF - 4:
                        te.wait_ge(t_free[1], FILL_ACT[l] + NFB)
                    product(LAP_DOWN[l] + 3 * b, u, hT_hi, hT_lo, k0, tiles, job % 2, u == 0, u == UF - 1)
                    if u == 2 and first:
                        te.wait_ge(job_out, job)
                        turn(act, FILL_ACT[l] + NFB - 1)
                    if u == 2 and not first and l == 0:
                        te.wait_ge(job_out, job)
                        turn(hblk, FILL_DOWN + b - 1)

            gate_up(0, 0, True)
            with te.Fori(1, NFB) as j:
                gate_up(0, j, False)
            down(0, 0, True)
            with te.Fori(1, NBLK) as b:
                down(0, b, False)

            pair_free(JOB_KV)
            for u, (k0, tiles, _) in enumerate(UNITS_D):
                if u % 2 == 0:
                    te.wait_ge(t_free[1], FILL_DOWN + u // 2 + 1)
                product(LAP_KV, u, xT_hi, xT_lo, k0, tiles, JOB_KV % 2, u == 0, u == UD - 1)
                if u == 2:
                    te.wait_ge(job_out, JOB_KV)
                    turn(hblk, FILL_DOWN + 3)

            def q_turn(g, t):
                for b in range(2):
                    te.wait_ge(t_free[b], FILL_G + 6 * g + t)
                    for a in range(4):
                        head = 4 * b + a
                        last = nc.tensor.transpose(acc[0:DH, TURN + b, a * P:(a + 1) * P],
                                                   q[:, t, head * DH:(head + 1) * DH], ident[:, :])
                    last.then_inc(t_full[b], 1)

            def scores(g, n):
                item, e = NCH * g + n, n % 2
                keys = CHUNK if n == 0 else 2 * CHUNK
                window = max(n - 1, 0)
                if item >= 2:
                    te.wait_ge(p_exp, item - 1)
                for j in range(PAIRS):
                    last = nc.tensor.matmul(acc[:, WORK + e, j * P:j * P + keys],
                                            qT[:, n, 2 * j:2 * j + 2, :].rearrange("d h s -> d (h s)"),
                                            kT[:, g, window, 0:keys], start=True, stop=True)
                last.then_inc(s_full, 1)

            def prob_turn(g, half):
                for e in range(2):
                    n = 2 * half + e
                    keys = CHUNK if n == 0 else 2 * CHUNK
                    te.wait_ge(p_norm, NCH * g + n + 1)
                    te.wait_ge(t_free[e], FILL_G + 6 * g + 2 + 2 * half)
                    for j in range(PAIRS):
                        last = nc.tensor.transpose(acc[0:keys, TURN + e, j * P:(j + 1) * P],
                                                   prob[:, e, j, 0:keys], ident[:, :])
                    last.then_inc(t_full[e], 1)

            def values(g, half):
                for e in range(2):
                    n = 2 * half + e
                    keys = CHUNK if n == 0 else 2 * CHUNK
                    te.wait_ge(t_free[e], FILL_G + 6 * g + 3 + 2 * half)
                    cols = slice(g * DH, (g + 1) * DH)
                    vcols = slice((GROUPS + g) * DH, (GROUPS + g + 1) * DH)
                    v = [kv[0:CHUNK, 0, vcols], kv[:, 0, vcols], v_mid[:, cols], kv[:, 1, vcols]][n]
                    for hh in range(2):
                        last = nc.tensor.matmul(acc[hh * DH:(hh + 1) * DH, TURN + e, 0:PAIRS * CHUNK], v,
                                                probT[0:keys, e, :, hh * CHUNK:(hh + 1) * CHUNK],
                                                start=True, stop=True)
                    last.then_inc(t_full[e], 1)

            def attention_step(g, s):
                if s == 2:
                    te.wait_ge(q_ready, g + 1)
                    q_turn(g, 0)
                if s == 3:
                    q_turn(g, 1)
                if s == 4:
                    for b in range(2):
                        te.wait_ge(t_free[b], FILL_G + 6 * g + 2)
                    scores(g, 0)
                    scores(g, 1)
                if s == 5:
                    scores(g, 2)
                if s == 6:
                    scores(g, 3)
                    prob_turn(g, 0)
                if s == 7:
                    values(g, 0)
                if s == 8:
                    prob_turn(g, 1)
                if s == 9:
                    values(g, 1)

            for g in range(GROUPS):
                pair_free(JOB_Q + g)
                for u, (k0, tiles, _) in enumerate(UNITS_D):
                    product(LAP_Q + g, u, xT_hi, xT_lo, k0, tiles, (JOB_Q + g) % 2, u == 0, u == UD - 1)
                    if g == 0 and u == 3:
                        te.wait_ge(kv_ready, 1)
                        for t in range(T):
                            te.wait_ge(t_free[t], FILL_K)
                            for a in range(GROUPS):
                                last = nc.tensor.transpose(acc[0:DH, TURN + t, a * P:(a + 1) * P],
                                                           kv[:, t, a * DH:(a + 1) * DH], ident[:, :])
                            last.then_inc(t_full[t], 1)
                    if g >= 2 and u < 2:
                        attention_step(g - 2, u + 8)
                    if g >= 1 and u >= 2:
                        attention_step(g - 1, u)
            for n, (job, u) in enumerate(O_FIRST):
                if u == 0:
                    pair_free(JOB_O + job)
                if n == 0:
                    te.wait_ge(t_free[1], FILL_G + 6 * 1 + 6)
                if u == 4 and job == 0:
                    te.wait_ge(t_free[1], FILL_G + 6 * 2 + 6)
                if n == 12:
                    te.wait_ge(t_free[1], FILL_G + 6 * 3 + 6)
                k0, tiles, _ = UNITS_D[u]
                product(LAP_O, n, oT_hi, oT_lo, k0, tiles, (JOB_O + job) % 2, u == 0, u == UD - 1)
                if n < 2:
                    attention_step(2, n + 8)
                elif n < 10:
                    attention_step(3, n)
            for b in range(2, NBLK):
                pair_free(JOB_O + b)
                for u, (k0, tiles, _) in enumerate(UNITS_D):
                    product(LAP_O + b, u, oT_hi, oT_lo, k0, tiles, (JOB_O + b) % 2, u == 0, u == UD - 1)
                    c = {(2, 0): 0, (2, 3): 1, (3, 2): 2}.get((b, u))
                    if c is not None:
                        te.wait_ge(job_out, JOB_O + c + 1)
                        turn(hblk, FILL_O + c)

            gate_up(1, 0, True)
            with te.Fori(1, NFB) as j:
                gate_up(1, j, False)
            down(1, 0, True)
            with te.Fori(1, NBLK - 1) as b:
                down(1, b, False)
            pair_free(JOB_DOWN[1] + NBLK - 1)
            order = [(u, range(T)) for u in range(UF - RING)]
            order += [(u, [t]) for t in range(T) for u in range(UF - RING, UF)]
            for u, tokens in order:
                k0, tiles, _ = UNITS_F[u]
                last = product(LAP_DOWN[1] + 3 * (NBLK - 1), u, hT_hi, hT_lo, k0, tiles,
                               (JOB_DOWN[1] + NBLK - 1) % 2, u == 0, u == UF - 1, tokens)
                if u == UF - 1 and 0 in tokens:
                    last.then_inc(tile0_done, 1)

        @block.gpsimd
        def _(gp):
            nc.gpsimd.memset(pick[:, :, :], 0.0).then_inc(ident_ready, 1)
            gp.wait_ge(ident_ready, 1)
            nc.gpsimd.affine_select(out=pick[:, :, :], in_=pick[:, :, :], compare_op=ALU.not_equal, fill=1.0,
                                    base=0, pattern=[[-1, NBLK], [0, P]],
                                    channel_multiplier=1).then_inc(ident_ready, 1)
            nc.gpsimd.memset(ident[:, :], 0.0).then_inc(ident_ready, 1)
            gp.wait_ge(ident_ready, 3)
            nc.gpsimd.affine_select(out=ident[:, :], in_=ident[:, :], compare_op=ALU.not_equal, fill=1.0,
                                    base=0, pattern=[[-1, P]], channel_multiplier=1).then_inc(ident_ready, 1)
            for piece in x_in:
                gp.wait_ge(piece, 16)
            for c in range(NBLK):
                cols = slice(c * C, (c + 1) * C)
                gp.wait_ge(bias_ready, c + 1)
                nc.gpsimd.tensor_tensor(xb[:, :, cols], h[:, :, cols],
                                        bias_b[:, cols].unsqueeze(1).to_broadcast([P, T, C]),
                                        ALU.add).then_inc(xb_ready, 1)
            gp.wait_ge(small_in, 32)
            nc.gpsimd.tensor_scalar(nsink[:, :], sink[:, :], -1.0, None, ALU.mult).then_inc(ident_ready, 1)

            def store(job, c):
                gp.wait_ge(job_out, job + 1)
                nc.gpsimd.tensor_copy(h[:, :, bass.ds(c * C, C)], hblk[:, :, :]).then_inc(h_stored, 1)

            for g in range(NBLK):
                gp.wait_ge(mix_full, 2 * g + 2)
                store(g, g)
            with gp.Fori(0, NBLK) as b:
                store(JOB_DOWN[0] + b, b)

            def rotate(z, heads, n):
                half = ROT // 2
                for t in range(T):
                    zt = z[:, t, 0:heads * DH].rearrange("p (h d) -> p h d", h=heads)
                    cos = ropes[:, 0, t, :].unsqueeze(1).to_broadcast([P, heads, ROT])
                    sin = ropes[:, 1, t, :].unsqueeze(1).to_broadcast([P, heads, ROT])
                    a, b = rope_a[:, t, 0:heads, :], rope_b[:, t, 0:heads, :]
                    nc.gpsimd.tensor_tensor(a, zt[:, :, 0:ROT], cos, ALU.mult)
                    nc.gpsimd.tensor_tensor(b[:, :, 0:half], zt[:, :, half:ROT], sin[:, :, 0:half], ALU.mult)
                    last = nc.gpsimd.tensor_tensor(b[:, :, half:], zt[:, :, 0:half], sin[:, :, half:], ALU.mult)
                last.then_inc(rope_step, 1)
                gp.wait_ge(rope_step, n + 1)
                for t in range(T):
                    zt = z[:, t, 0:heads * DH].rearrange("p (h d) -> p h d", h=heads)
                    last = nc.gpsimd.tensor_tensor(zt[:, :, 0:ROT], rope_a[:, t, 0:heads, :],
                                                   rope_b[:, t, 0:heads, :], ALU.add)
                return last

            gp.wait_ge(job_out, JOB_KV + 1)
            rotate(kv, GROUPS, 0).then_inc(kv_ready, 1)
            for g in range(GROUPS):
                gp.wait_ge(job_out, JOB_Q + g + 1)
                rotate(q, HPG, g + 1).then_inc(q_ready, 1)
            with gp.Fori(0, NBLK) as b:
                store(JOB_O + b, b)
            gp.wait_ge(gfin_in, 16)
            with gp.Fori(0, NBLK - 1) as b:
                gp.wait_ge(job_out, JOB_DOWN[1] + b + 1)
                nc.gpsimd.tensor_tensor(h[:, :, bass.ds(b * C, C)], hblk[:, :, :],
                                        gfin[:, bass.ds(b * C, C)].unsqueeze(1).to_broadcast([P, T, C]),
                                        ALU.mult).then_inc(h_stored, 1)


def band_matrices():
    m = np.zeros((P, len(WINDOWS), BANDW + P), np.float32)
    for g, w in enumerate(WINDOWS):
        for t in range(P):
            for s in range(t, t + w):
                m[t, g, s] = np.float32(1) / np.float32(min(s + 1, w))
                if s < P:
                    m[t, g, BANDW + s] = np.float32(1) / np.float32(w)
            m[t, g, t] -= np.float32(1)
            m[t, g, BANDW + t] -= np.float32(1)
    return m


def rope_tables():
    half = ROT // 2
    inv = np.float32(THETA) ** (-np.arange(half, dtype=np.float32) * np.float32(2.0) / np.float32(ROT))
    ang = (np.arange(S, dtype=np.float32)[:, None] * inv.astype(np.float32)[None, :]).astype(np.float32)
    cos, sin = np.cos(ang.astype(np.float64)), np.sin(ang.astype(np.float64))
    both = np.stack([np.concatenate([cos, cos], 1), np.concatenate([-sin, sin], 1)]).astype(np.float32)
    return np.ascontiguousarray(both.reshape(2, T, P, ROT).transpose(2, 0, 1, 3))


def kernel(x, pool_norm, pool_w, pool_b, pool_scale, kv_norm, w_kv, attn_norm, w_q, sinks, w_o,
           ffn_norm, w_gate, w_up, w_down, final_norm):
    import concourse.bacc as bacc
    from concourse.bass_utils import run_bass_kernel_spmd

    gains = [pool_norm[0], ffn_norm[0], ffn_norm[1], kv_norm, attn_norm[0]]
    by_head = np.asarray(sinks).reshape(GROUPS * PAIRS, 2).T
    arrays = {
        "x": x, "pool_w": pool_w,
        "pool_rows": np.stack([np.asarray(v).reshape(NBLK, C) for v in (pool_scale, pool_b)], axis=1),
        "w_kv": w_kv, "w_q": w_q, "w_o": w_o, "w_gate": w_gate, "w_up": w_up, "w_down": w_down,
        "final_norm": np.asarray(final_norm).reshape(1, D),
        "gain_cols": np.stack([np.asarray(g).reshape(KD, P).T for g in gains], axis=1),
        "sink_rows": np.repeat(by_head, CHUNK, axis=0),
        "bands": band_matrices(), "rope": rope_tables(),
    }
    arrays = {n + "_in": np.ascontiguousarray(a) for n, a in arrays.items()}
    nc = bacc.Bacc("TRN2", target_bir_lowering=False, num_devices=1)
    args = {n[:-3]: nc.dram_tensor(n, a.shape, mybir.dt.from_np(a.dtype), kind="ExternalInput").ap()
            for n, a in arrays.items()}
    args["final_norm"] = args["final_norm"][0]
    out = nc.dram_tensor("out", (1, S, D), F32, kind="ExternalOutput").ap()
    trunk(nc, out=out, **args)
    return run_bass_kernel_spmd(nc, [arrays], core_ids=[0]).results[0]["out"]
```
